# Optimizing a Trainium2 kernel written in Bass

```python
import jax, jax.numpy as jnp
from jax import lax
import numpy as np

D_MODEL = 2048
BATCH = 1
SEQ = 256
DEPTH = 2

CHUNK = 64
RMS_EPS = 1e-6
NEG_INF = -1e30

A_HEADS = 16
A_KV_HEADS = 4
A_HEAD_DIM = 64
A_WINDOW = 128
A_WIN_CHUNKS = A_WINDOW // CHUNK
A_Q = A_HEADS * A_HEAD_DIM
A_KV = A_KV_HEADS * A_HEAD_DIM

B_HEADS = 4
B_QK_DIM = 128
B_V_DIM = 256
B_CONV = 4
B_QK = B_HEADS * B_QK_DIM
B_V = B_HEADS * B_V_DIM

C_HEADS = 16
C_HEAD_DIM = 64
C_LEFT_CHUNKS = 8
C_REL_CLIP = 128
C_W = C_HEADS * C_HEAD_DIM

D_HEADS = 8
D_QK_DIM = 128
D_V_DIM = 128
D_QK = D_HEADS * D_QK_DIM
D_V = D_HEADS * D_V_DIM
ROPE_BASE = 10000.0

FFN_HIDDEN = -(-8 * D_MODEL // (3 * 256)) * 256

EVEN_SIZES = (A_Q, A_KV, A_KV, B_QK, B_QK, B_V, B_V, B_HEADS, B_HEADS)
ODD_SIZES = (C_W, C_W, C_W, D_QK, D_QK, D_V, D_V)
EVEN_IN = sum(EVEN_SIZES)
ODD_IN = sum(ODD_SIZES)
EVEN_OUT = A_Q + B_V
ODD_OUT = C_W + D_V
N_EVEN = (DEPTH + 1) // 2
N_ODD = DEPTH // 2

kernel_name = 'hybrid_swa_mlstm_chunkrel_retention_block'

def rmsnorm(x, g):
    xf = x.astype(jnp.float32)
    y = xf * lax.rsqrt(jnp.mean(xf * xf, axis=-1, keepdims=True) + RMS_EPS)
    return (y * g.astype(jnp.float32)).astype(x.dtype)

def head_norm(h, g, n_heads):
    bsz, seq, width = h.shape
    hh = h.reshape(bsz, seq, n_heads, width // n_heads)
    mu = jnp.mean(hh, axis=-1, keepdims=True)
    var = jnp.mean(jnp.square(hh - mu), axis=-1, keepdims=True)
    y = (hh - mu) * lax.rsqrt(var + RMS_EPS)
    return y.reshape(bsz, seq, width) * g.astype(jnp.float32)

def split_cols(p, sizes):
    out, start = [], 0
    for s in sizes:
        out.append(p[..., start:start + s])
        start += s
    return out

def to_heads_chunks(t, n_heads, d):
    bsz, seq, _ = t.shape
    return t.reshape(bsz, seq // CHUNK, CHUNK, n_heads, d).transpose(0, 3, 1, 2, 4)

def gates_to_chunks(t):
    bsz, seq, nh = t.shape
    return t.reshape(bsz, seq // CHUNK, CHUNK, nh).transpose(0, 3, 1, 2)

def from_heads_chunks(t):
    bsz, nh, nc, l, d = t.shape
    return t.transpose(0, 2, 3, 1, 4).reshape(bsz, nc * l, nh * d)

def chunk_band(t, n):
    nc = t.shape[1]
    tp = jnp.pad(t, [(0, 0), (n - 1, 0)] + [(0, 0)] * (t.ndim - 2))
    return jnp.concatenate([tp[:, j:j + nc] for j in range(n)], axis=2)

def causal_dwconv(x, w, b):
    ch = x.shape[-1]
    y = lax.conv_general_dilated(x, w[:, None, :].astype(x.dtype), window_strides=(1,),
                                 padding=[(w.shape[0] - 1, 0)],
                                 dimension_numbers=('NWC', 'WIO', 'NWC'),
                                 feature_group_count=ch)
    return y + b.astype(x.dtype)

def rotary(t, n_heads, d):
    bsz, seq, _ = t.shape
    t = t.reshape(bsz, seq, n_heads, d)
    inv = ROPE_BASE ** (-jnp.arange(0, d, 2, dtype=jnp.float32) / d)
    ang = jnp.arange(seq, dtype=jnp.float32)[:, None] * inv[None, :]
    cos = jnp.cos(ang)[None, :, None, :]
    sin = jnp.sin(ang)[None, :, None, :]
    t1, t2 = t[..., :d // 2], t[..., d // 2:]
    return jnp.concatenate([t1 * cos - t2 * sin, t1 * sin + t2 * cos], axis=-1).reshape(bsz, seq, n_heads * d)

def sliding_window_sink_attention(q, k, v, sinks):
    bsz, seq, _ = q.shape
    nc = seq // CHUNK
    grp = A_HEADS // A_KV_HEADS
    q = q.reshape(bsz, nc, CHUNK, A_KV_HEADS, grp, A_HEAD_DIM)
    k = k.reshape(bsz, nc, CHUNK, A_KV_HEADS, A_HEAD_DIM)
    v = v.reshape(bsz, nc, CHUNK, A_KV_HEADS, A_HEAD_DIM)
    k_band = chunk_band(k, A_WIN_CHUNKS)
    v_band = chunk_band(v, A_WIN_CHUNKS)
    s = jnp.einsum('bcqkgd,bcskd->bckgqs', q, k_band).astype(jnp.float32) * (A_HEAD_DIM ** -0.5)
    key_chunk = (jnp.arange(nc)[:, None] - (A_WIN_CHUNKS - 1)
                 + jnp.arange(A_WIN_CHUNKS * CHUNK)[None, :] // CHUNK)
    valid = (key_chunk >= 0)[None, :, None, None, None, :]
    s = jnp.where(valid, s, NEG_INF)
    sink = jnp.broadcast_to(
        sinks.astype(jnp.float32).reshape(A_KV_HEADS, grp)[None, None, :, :, None, None],
        s.shape[:-1] + (1,))
    p = jax.nn.softmax(jnp.concatenate([s, sink], axis=-1), axis=-1)[..., :-1]
    o = jnp.einsum('bckgqs,bcskd->bcqkgd', p.astype(v.dtype), v_band)
    return o.reshape(bsz, seq, A_Q)

def mlstm(q, k, v, i_pre, f_pre, o_pre, norm_g):
    f32 = jnp.float32
    bsz = q.shape[0]
    q = to_heads_chunks(q.astype(f32), B_HEADS, B_QK_DIM)
    k = to_heads_chunks(k.astype(f32), B_HEADS, B_QK_DIM) * (B_QK_DIM ** -0.5)
    v = to_heads_chunks(v.astype(f32), B_HEADS, B_V_DIM)
    ig = gates_to_chunks(i_pre.astype(f32))
    logf = jax.nn.log_sigmoid(gates_to_chunks(f_pre.astype(f32)))
    b = jnp.cumsum(logf, axis=-1)
    b_last = b[..., -1]
    a = b_last[..., None] - b + ig
    m_loc = jnp.max(a, axis=-1)
    w = jnp.exp(a - m_loc[..., None])
    c_loc = jnp.einsum('bhcs,bhcsv,bhcsd->bhcvd', w, v, k)
    n_loc = jnp.einsum('bhcs,bhcsd->bhcd', w, k)

    def step(carry, inp):
        c_st, n_st, m_st = carry
        bl, ml, cl, nl = inp
        m_new = jnp.maximum(bl + m_st, ml)
        s_prev = jnp.exp(bl + m_st - m_new)
        s_loc = jnp.exp(ml - m_new)
        c_new = s_prev[..., None, None] * c_st + s_loc[..., None, None] * cl
        n_new = s_prev[..., None] * n_st + s_loc[..., None] * nl
        return (c_new, n_new, m_new), (c_st, n_st, m_st)

    init = (jnp.zeros((bsz, B_HEADS, B_V_DIM, B_QK_DIM), f32),
            jnp.zeros((bsz, B_HEADS, B_QK_DIM), f32),
            jnp.zeros((bsz, B_HEADS), f32))
    xs = (jnp.moveaxis(b_last, 2, 0), jnp.moveaxis(m_loc, 2, 0),
          jnp.moveaxis(c_loc, 2, 0), jnp.moveaxis(n_loc, 2, 0))
    _, (c_prev, n_prev, m_prev) = lax.scan(step, init, xs)
    c_prev = jnp.moveaxis(c_prev, 0, 2)
    n_prev = jnp.moveaxis(n_prev, 0, 2)
    m_prev = jnp.moveaxis(m_prev, 0, 2)

    g = b + m_prev[..., None]
    causal = jnp.tril(jnp.ones((CHUNK, CHUNK), dtype=bool))
    d_log = jnp.where(causal, b[..., :, None] - b[..., None, :] + ig[..., None, :], -jnp.inf)
    m_t = jnp.maximum(g, jnp.max(d_log, axis=-1))
    scores = jnp.einsum('bhctd,bhcsd->bhcts', q, k) * jnp.exp(d_log - m_t[..., None])
    inter = jnp.exp(g - m_t)
    num = (jnp.einsum('bhcts,bhcsv->bhctv', scores, v)
           + inter[..., None] * jnp.einsum('bhctd,bhcvd->bhctv', q, c_prev))
    den = jnp.sum(scores, axis=-1) + inter * jnp.einsum('bhctd,bhcd->bhct', q, n_prev)
    h = num / jnp.maximum(jnp.abs(den), jnp.exp(-m_t))[..., None]
    h = from_heads_chunks(h)
    return head_norm(h, norm_g, B_HEADS) * jax.nn.sigmoid(o_pre.astype(f32))

def chunked_relpos_attention(q, k, v, rel_table):
    bsz, seq, _ = q.shape
    nc = seq // CHUNK
    band = (C_LEFT_CHUNKS + 1) * CHUNK
    pad = C_LEFT_CHUNKS * CHUNK
    q = q.reshape(bsz, seq, C_HEADS, C_HEAD_DIM)
    k_pad = jnp.pad(k.reshape(bsz, seq, C_HEADS, C_HEAD_DIM), ((0, 0), (pad, 0), (0, 0), (0, 0)))
    v_pad = jnp.pad(v.reshape(bsz, seq, C_HEADS, C_HEAD_DIM), ((0, 0), (pad, 0), (0, 0), (0, 0)))
    i = jnp.arange(CHUNK)[:, None]
    j = jnp.arange(band)[None, :]
    dist = pad + i - j
    idx = jnp.clip(dist, -C_REL_CLIP, C_REL_CLIP) + C_REL_CLIP
    bias = rel_table.astype(jnp.float32)[:, idx]
    scale = C_HEAD_DIM ** -0.5

    def one_chunk(c):
        start = c * CHUNK
        qc = lax.dynamic_slice_in_dim(q, start, CHUNK, axis=1)
        kc = lax.dynamic_slice_in_dim(k_pad, start, band, axis=1)
        vc = lax.dynamic_slice_in_dim(v_pad, start, band, axis=1)
        s = jnp.einsum('bqhd,bkhd->bhqk', qc, kc).astype(jnp.float32) * scale + bias
        valid = (start + j - pad) >= 0
        s = jnp.where(valid, s, NEG_INF)
        p = jax.nn.softmax(s, axis=-1)
        return jnp.einsum('bhqk,bkhd->bqhd', p.astype(vc.dtype), vc)

    out = lax.map(one_chunk, jnp.arange(nc))
    return out.transpose(1, 0, 2, 3, 4).reshape(bsz, seq, C_W)

def retention(q, k, v, g_pre, norm_g):
    f32 = jnp.float32
    q = to_heads_chunks(rotary(q.astype(f32), D_HEADS, D_QK_DIM), D_HEADS, D_QK_DIM)
    k = to_heads_chunks(rotary(k.astype(f32), D_HEADS, D_QK_DIM), D_HEADS, D_QK_DIM) * (D_QK_DIM ** -0.5)
    v = to_heads_chunks(v.astype(f32), D_HEADS, D_V_DIM)
    bsz = q.shape[0]
    log_gamma = jnp.log1p(-jnp.exp2(-5.0 - jnp.arange(D_HEADS, dtype=f32)))
    pos = jnp.arange(CHUNK, dtype=f32)
    rel = pos[:, None] - pos[None, :]
    decay = jnp.where(rel >= 0, jnp.exp(log_gamma[:, None, None] * jnp.maximum(rel, 0.0)), 0.0)
    xi = jnp.exp(log_gamma[:, None] * (pos + 1.0))
    zeta = jnp.exp(log_gamma[:, None] * (CHUNK - 1.0 - pos))
    chunk_decay = jnp.exp(log_gamma * CHUNK)
    r_loc = jnp.einsum('bhcsd,hs,bhcsv->bhcdv', k, zeta, v)

    def step(r, r_c):
        return chunk_decay[None, :, None, None] * r + r_c, r

    _, r_prev = lax.scan(step, jnp.zeros((bsz, D_HEADS, D_QK_DIM, D_V_DIM), f32),
                         jnp.moveaxis(r_loc, 2, 0))
    r_prev = jnp.moveaxis(r_prev, 0, 2)
    inner = jnp.einsum('bhctd,bhcsd->bhcts', q, k) * decay[None, :, None]
    o = (jnp.einsum('bhcts,bhcsv->bhctv', inner, v)
         + xi[None, :, None, :, None] * jnp.einsum('bhctd,bhcdv->bhctv', q, r_prev))
    o = head_norm(from_heads_chunks(o), norm_g, D_HEADS)
    return o * jax.nn.silu(g_pre.astype(f32))

def even_mixer(h, w_in, sinks, conv_w, conv_b, ig_bias, fg_bias, norm_g, w_out):
    aq, ak, av, bq, bk, bv, bo, bi, bf = split_cols(h @ w_in, EVEN_SIZES)
    bqk = jax.nn.silu(causal_dwconv(jnp.concatenate([bq, bk], axis=-1), conv_w, conv_b))
    bq, bk = bqk[..., :B_QK], bqk[..., B_QK:]
    ya = sliding_window_sink_attention(aq, ak, av, sinks)
    yb = mlstm(bq, bk, bv,
               bi.astype(jnp.float32) + ig_bias.astype(jnp.float32),
               bf.astype(jnp.float32) + fg_bias.astype(jnp.float32),
               bo, norm_g)
    return jnp.concatenate([ya, yb.astype(h.dtype)], axis=-1) @ w_out

def odd_mixer(h, w_in, rel_bias, norm_g, w_out):
    cq, ck, cv, dq, dk, dv, dg = split_cols(h @ w_in, ODD_SIZES)
    yc = chunked_relpos_attention(cq, ck, cv, rel_bias)
    yd = retention(dq, dk, dv, dg, norm_g)
    return jnp.concatenate([yc, yd.astype(h.dtype)], axis=-1) @ w_out

def swiglu(h, w_gate, w_up, w_down):
    return (jax.nn.silu(h @ w_gate) * (h @ w_up)) @ w_down

def setup_inputs(seed: int = 0) -> dict:
    key = jax.random.key(seed)
    ks = jax.random.split(key, 20)
    f32 = jnp.float32

    def dense(k, shape, fan_in):
        return jax.random.normal(k, shape, f32) * (fan_in ** -0.5)

    def gain(k, shape):
        return 1.0 + 0.02 * jax.random.normal(k, shape, f32)

    fgate = (jnp.linspace(3.0, 6.0, B_HEADS, dtype=f32)[None, :]
             + 0.1 * jax.random.normal(ks[9], (N_EVEN, B_HEADS), f32))
    return {
        'x': jax.random.normal(ks[0], (BATCH, SEQ, D_MODEL), f32),
        'ln_mix_g': gain(ks[1], (DEPTH, D_MODEL)),
        'ln_ffn_g': gain(ks[2], (DEPTH, D_MODEL)),
        'even_w_in': dense(ks[3], (N_EVEN, D_MODEL, EVEN_IN), D_MODEL),
        'even_w_out': dense(ks[4], (N_EVEN, EVEN_OUT, D_MODEL), EVEN_OUT),
        'a_sinks': jax.random.normal(ks[5], (N_EVEN, A_HEADS), f32),
        'b_conv_w': dense(ks[6], (N_EVEN, B_CONV, 2 * B_QK), B_CONV),
        'b_conv_b': 0.02 * jax.random.normal(ks[7], (N_EVEN, 2 * B_QK), f32),
        'b_igate_bias': 0.1 * jax.random.normal(ks[8], (N_EVEN, B_HEADS), f32),
        'b_fgate_bias': fgate,
        'b_norm_g': gain(ks[10], (N_EVEN, B_V)),
        'odd_w_in': dense(ks[11], (N_ODD, D_MODEL, ODD_IN), D_MODEL),
        'odd_w_out': dense(ks[12], (N_ODD, ODD_OUT, D_MODEL), ODD_OUT),
        'c_rel_bias': 0.5 * jax.random.normal(ks[13], (N_ODD, C_HEADS, 2 * C_REL_CLIP + 1), f32),
        'd_norm_g': gain(ks[14], (N_ODD, D_V)),
        'ffn_w_gate': dense(ks[15], (DEPTH, D_MODEL, FFN_HIDDEN), D_MODEL),
        'ffn_w_up': dense(ks[16], (DEPTH, D_MODEL, FFN_HIDDEN), D_MODEL),
        'ffn_w_down': dense(ks[17], (DEPTH, FFN_HIDDEN, D_MODEL), FFN_HIDDEN),
        'final_g': gain(ks[18], (D_MODEL,)),
    }

def reference(x, ln_mix_g, ln_ffn_g, even_w_in, even_w_out, a_sinks, b_conv_w, b_conv_b,
              b_igate_bias, b_fgate_bias, b_norm_g, odd_w_in, odd_w_out, c_rel_bias, d_norm_g,
              ffn_w_gate, ffn_w_up, ffn_w_down, final_g):
    for layer in range(DEPTH):
        h = rmsnorm(x, ln_mix_g[layer])
        if layer % 2 == 0:
            e = layer // 2
            x = x + even_mixer(h, even_w_in[e], a_sinks[e], b_conv_w[e], b_conv_b[e],
                               b_igate_bias[e], b_fgate_bias[e], b_norm_g[e], even_w_out[e])
        else:
            o = layer // 2
            x = x + odd_mixer(h, odd_w_in[o], c_rel_bias[o], d_norm_g[o], odd_w_out[o])
        h = rmsnorm(x, ln_ffn_g[layer])
        x = x + swiglu(h, ffn_w_gate[layer], ffn_w_up[layer], ffn_w_down[layer])
    return rmsnorm(x, final_g)


_drawn_inputs = setup_inputs


def setup_inputs(seed=0):
    import zlib

    import numpy as np

    out = dict(_drawn_inputs(seed))
    spreads = {}
    factors = {'a_sinks': 8.0,
     'b_conv_b': 5.86,
     'b_igate_bias': 23.699,
     'b_norm_g': 4.106,
     'd_norm_g': 25.644,
     'final_g': 8.069,
     'c_rel_bias': 4.697}
    for name, (base, spread) in spreads.items():
        noise = np.random.default_rng([zlib.crc32(name.encode()), seed]).standard_normal(out[name].shape)
        drawn = base * np.exp(spread * noise) if base else spread * noise
        out[name] = __import__('jax').numpy.asarray(drawn.astype(out[name].dtype))
    for name, factor in factors.items():
        out[name] = (out[name] * factor).astype(out[name].dtype)
    return out
```

```python
import concourse.bass as bass
from concourse import mybir
from contextlib import ExitStack

import numpy as np

F32 = mybir.dt.float32
F32R = mybir.dt.float32r
BF16 = mybir.dt.bfloat16
ALU = mybir.AluOpType
ACT = mybir.ActivationFunctionType
AX = mybir.AxisListType

P = 128
S = 256
TT = S // P
D = 2048
KT = D // P
CW = 512
EPS = 1e-6
NEG = -1e30
FF = 5632
FKT = FF // P
FCH = FF // CW
EVEN_IN, ODD_IN = 4616, 7168
NCH = D // CW

E_ORDER = [2, 0, 1, 3, 4, 5, 6, 7, 8]
O_ORDER = [0, 2, 1, 3, 4, 5, 6, 8, 7, 9, 10, 11, 12, 13]
UNITS_IN = [4] * 4
UNITS_DOWN = [4] * 8 + [3] * 4
STARTS_DOWN = [sum(UNITS_DOWN[:i]) for i in range(len(UNITS_DOWN))]

U_E = 0
U_EO = U_E + 4 * len(E_ORDER)
U_F0 = U_EO + 4 * NCH
U_D0 = U_F0 + 8 * FCH
U_O = U_D0 + 12 * NCH
U_OO = U_O + 4 * len(O_ORDER)
U_F1 = U_OO + 4 * NCH
U_D1 = U_F1 + 8 * FCH
UNITS = U_D1 + 12 * NCH
UNIT_ROWS = [4] * U_D0 + UNITS_DOWN * NCH + [4] * (U_D1 - U_O) + UNITS_DOWN * NCH
C_E = 0
C_EO = len(E_ORDER)
C_F0 = C_EO + NCH
C_D0 = C_F0 + 2 * FCH
C_O = C_D0 + NCH
C_OO = C_O + len(O_ORDER)
C_F1 = C_OO + NCH
C_D1 = C_F1 + 2 * FCH

E_TURNS = sorted(
    [(4 + i, "k", i) for i in range(4)] + [(8 + i, "q", i) for i in range(8)]
    + [(17 + 2 * i, "conv", i) for i in range(8)]
    + [(16 + 2 * i, "y", i) for i in range(8)]
    + [(36, "y", 8), (36, "y", 9), (36, "y", 10), (36, "y", 11)]
    + [(37, "y", 12), (37, "y", 13), (37, "y", 14), (37, "y", 15)])
RQK_SLOTS = [28, 30, 31, 33, 34, 36, 37, 39, 40, 42, 43, 45, 46, 47, 48, 49]
O_TURNS = sorted(
    [(4 + i, "q", i) for i in range(4)] + [(8 + i, "k", i) for i in range(4)]
    + [(12 + i, "q", 4 + i) for i in range(4)] + [(16 + i, "k", 4 + i) for i in range(4)]
    + [(s, "rope", i) for i, s in enumerate(RQK_SLOTS)]
    + [(23 + 3 * i, "y", i) for i in range(8)]
    + [(52 + i, "y", 8 + i) for i in range(4)]
    + [(56, "y", 12), (56, "y", 13), (57, "y", 14), (57, "y", 15)])
T_X = 0
T_E = T_X + KT
T_EO = T_E + len(E_TURNS)
T_F0 = T_EO + KT
T_D0 = T_F0 + FKT
T_O = T_D0 + KT
T_OO = T_O + len(O_TURNS)
T_F1 = T_OO + KT

E_ATT = [13 + 2 * k for k in range(8)]
O_ATT = [20 + 3 * k for k in range(8)]
E_MLSTM = [29, 30, 31, 33]
O_RET = [44, 45, 46, 47, 50, 51, 52, 53]
LATE = 36, 56

MLSTM_SCALE = 128.0 ** -0.5 * 0.25


def turn_of(turns, base, kind, i):
    return base + [t[1:] for t in turns].index((kind, i))


def drains_before(chunk):
    return 2 * (chunk // 2)


def drains_after(chunk):
    return 2 * (chunk // 2) + 2


def half_rows(h):
    return min(2, UNIT_ROWS[h // 2] - 2 * (h % 2))


def split_ahead(split, u, j=0):
    for h in (2 * u + 3, 2 * u + 4):
        if h < 2 * UNITS:
            split(h, j)


def wait(eng, sem, value):
    if isinstance(value, int) and value <= 0:
        return
    eng.wait_ge(sem, value)


def build(nc, x, gains, final_g, w_e, w_eo, w_o, w_oo, w_gate, w_up, w_down, sinks, conv,
          gate_bias, b_norm_g, d_norm_g, rel, const, dtab, sel, out):
    ctx = ExitStack()
    with ctx:
        def sb(name, shape, dt=F32):
            return ctx.enter_context(nc.sbuf_tensor(name, shape, dt))

        def sem(name):
            return ctx.enter_context(nc.semaphore(name))

        xs = sb("xs", [P, TT, D])
        a_hi = sb("a_hi", [P, KT, S], F32R)
        a_lo = sb("a_lo", [P, KT, S], F32R)
        raw = sb("raw", [P, 4, 4, CW])
        w_hi = sb("w_hi", [P, 4, 2, CW], F32R)
        w_lo = sb("w_lo", [P, 4, 2, CW], F32R)
        ident = sb("ident", [P, P])
        ident_b = sb("ident_b", [P, P], BF16)
        gain = sb("gain", [P, 4, KT])
        ssq = sb("ssq", [P, 5, TT, NCH])
        ssum = sb("ssum", [P, 5, TT])
        root = sb("root", [P, 5, TT])
        rstd = sb("rstd", [P, 5, 3, TT])
        eps = sb("eps", [P, 1])
        ones = sb("ones", [P, P])
        junk = sb("junk", [P, CW], BF16)
        nm = sb("nm", [P, 2, 2])
        mx = sb("mx", [P, 2, 2])
        psum_p = sb("psum_p", [P, 2, 2])
        sinkv = sb("sinkv", [P, 8, 2, 2])
        nsink = sb("nsink", [P, 8, 2, 2])
        sshift = sb("sshift", [P, 2, 2])
        es = sb("es", [P, 2, 2])
        den = sb("den", [P, 2, 2])
        rden = sb("rden", [P, 2, 2])
        stats = sb("stats", [P, 8, TT, 6])
        mv = sb("mv", [P, 8, TT, 2])
        sd = sb("sd", [P, 8, TT])
        rs = sb("rs", [P, 8, TT])
        convp = sb("convp", [P, 8, 5])
        gbias = sb("gbias", [P, 8])

        base = -(-nc.sbuf_base // 64) * 64

        class Region:

            def __init__(self, at):
                self.at = at

            def put(self, name, shape, dt=F32, at=None):
                size = int(np.prod(shape[1:])) * (2 if dt == BF16 else 4)
                start = self.at if at is None else at
                if at is None:
                    self.at += -(-size // 32) * 32
                return nc.alloc_sbuf_tensor_at(name, shape, dt, offset=start), start

        ffn = Region(base)
        h_hi, _ = ffn.put("h_hi", [P, FKT, S], F32R)
        h_lo, _ = ffn.put("h_lo", [P, FKT, S], F32R)
        silu, _ = ffn.put("silu", [P, TT, CW])
        prod, _ = ffn.put("prod", [P, TT, CW])

        mix = Region(base)
        y_hi, _ = mix.put("y_hi", [P, KT, S], F32R)
        y_lo, _ = mix.put("y_lo", [P, KT, S], F32R)
        stage, _ = mix.put("stage", [P, 2, TT, CW])
        yp, _ = mix.put("yp", [P, TT, P])
        prob, prob_at = mix.put("prob", [P, 2, 384])
        probT, probT_at = mix.put("probT", [P, 2, 384])
        gfac, gfac_at = mix.put("gfac", [P, TT, 1024])
        split_at = mix.at

        ev = Region(split_at)
        aqT, aqT_at = ev.put("aqT", [P, 8, S])
        akT, _ = ev.put("akT", [P, 4, S])
        aknat, _ = ev.put("aknat", [P, TT, 4, 2, 64])
        av, _ = ev.put("av", [P, TT, 4 * 64])
        cbuf, _ = ev.put("cbuf", [P, 3 + S + 1])
        cacc, _ = ev.put("cacc", [P, 2, S])
        cth, _ = ev.put("cth", [P, S])
        mqk, _ = ev.put("mqk", [P, 8, S])
        mv_sb, _ = ev.put("mv_sb", [P, TT, 4, 260])
        gnorm, _ = ev.put("gnorm", [P, 1024])
        gw, _ = ev.put("gw", [P, KT, 8])
        gw_hi, _ = ev.put("gw_hi", [P, KT, 8], F32R)
        gw_lo, _ = ev.put("gw_lo", [P, KT, 8], F32R)
        upper, _ = ev.put("upper", [P, P])
        win_b, _ = ev.put("win_b", [P, 384], BF16)
        tri_b, _ = ev.put("tri_b", [P, P], BF16)
        selr, _ = ev.put("selr", [4, 4, P])
        negm, _ = ev.put("negm", [4, S])
        gx, _ = ev.put("gx", [P, TT, 8])
        gsc, _ = ev.put("gsc", [P, 8, TT, 4])
        yB, _ = ev.put("yB", [P, TT, 4, 256], at=aqT_at)
        cmax, _ = ev.put("cmax", [4, 2, P + S], at=prob_at)
        wgt, _ = ev.put("wgt", [P, 384], at=prob_at)
        scT, _ = ev.put("scT", [P, 384], at=prob_at + 1536)
        win_f, _ = ev.put("win_f", [P, 384 + P], at=probT_at)
        ev_end = ev.at

        od = Region(split_at - 8192)
        cqT, cqT_at = od.put("cqT", [P, 8, S], at=split_at)
        od.at = split_at + 8192
        ckT, ckT_at = od.put("ckT", [P, 8, S])
        cv, cv_at = od.put("cv", [P, TT, 1024])
        rqT, _ = od.put("rqT", [P, 8, S])
        rkT, _ = od.put("rkT", [P, 8, S])
        rv, _ = od.put("rv", [P, TT, 1024])
        rtmp, _ = od.put("rtmp", [P, 2, TT, 4, 64], at=gfac_at)
        biasT, _ = od.put("biasT", [P, 2, 2, S], at=gfac_at + 4096)
        trig, _ = od.put("trig", [P, 2, TT, 64])
        flip, _ = od.put("flip", [P, P])
        yD, _ = od.put("yD", [P, TT, 8, 128], at=cqT_at)
        decay, _ = od.put("decay", [P, 8, S], at=ckT_at)
        scD, _ = od.put("scD", [P, 2, 384], at=prob_at)
        gnorm_o, _ = od.put("gnorm_o", [P, 1024], at=cv_at)
        end = max(ffn.at, ev_end, od.at)
        assert end <= nc.sbuf_usable_end, (end, nc.sbuf_usable_end)
        ctx.enter_context(nc.sbuf_tensor("fence", [P, (end - nc.sbuf_base) // 4], F32))

        ps_g = ctx.enter_context(nc.psum_tensor("ps_g", [P, 2, TT, CW], F32))
        ps_s = ctx.enter_context(nc.psum_tensor("ps_s", [P, 2, CW], F32))
        ps_t = ctx.enter_context(nc.psum_tensor("ps_t", [P, 2, CW], F32))
        ring = [ps_s[:, 0, 0:S], ps_s[:, 1, 0:S], ps_t[:, 0, 0:S], ps_t[:, 1, 0:S]]
        ring = [r.rearrange("p (t c) -> p t c", t=TT) for r in ring]
        beside = ps_t[:, :, 384:512]
        region = {}
        n = 0
        for t0, turns in ((T_X, KT), (T_E, E_TURNS), (T_EO, KT), (T_F0, FKT), (T_D0, KT),
                          (T_O, O_TURNS), (T_OO, KT), (T_F1, FKT)):
            if isinstance(turns, int):
                for t in range(turns):
                    region[t0 + t] = (n + t) % 4
                n += turns
            else:
                late = LATE[t0 == T_O]
                for t, (slot, _, _) in enumerate(turns):
                    region[t0 + t] = "beside" if slot < late else n % 4
                    n += slot >= late

        def turn_psum(t):
            return beside if region[t] == "beside" else ring[region[t]]

        def banks(t):
            return {2, 3} if region[t] == "beside" else {region[t]}

        def turn_before(t):
            return max((u for u in range(t) if banks(u) & banks(t)), default=-1)

        params_in = sem("params_in")
        first_in = sem("first_in")
        x_in = [sem(f"x_in{n}") for n in range(NCH)]
        raw_in = [sem(f"raw_in{i}") for i in range(4)]
        hi_made = sem("hi_made")
        lo_made = sem("lo_made")
        half_used = sem("half_used")
        drained = [sem("drained0"), sem("drained1")]
        turned = sem("turned")
        turn_act = sem("turn_act")
        turn_dve = sem("turn_dve")
        squares = sem("squares")
        sum_made = sem("sum_made")
        root_made = sem("root_made")
        rstd_made = sem("rstd_made")
        consts_made = sem("consts_made")
        zeros_made = sem("zeros_made")
        scores_made = sem("scores_made")
        max_made = sem("max_made")
        probs_made = sem("probs_made")
        sinks_made = sem("sinks_made")
        probs_turned = sem("probs_turned")
        probT_act = sem("probT_act")
        probT_dve = sem("probT_dve")
        pv_made = sem("pv_made")
        pair_made = sem("pair_made")
        bias_in = [sem("bias_in0"), sem("bias_in1")]
        bias_masked = sem("bias_masked")
        gatew_hi = sem("gatew_hi")
        gatew_lo = sem("gatew_lo")
        gates_mm = sem("gates_mm")
        gates_dve = sem("gates_dve")
        gates_act = sem("gates_act")
        conv_made = sem("conv_made")
        tanh_made = sem("tanh_made")
        qk_made = sem("qk_made")
        ml_scores = sem("ml_scores")
        ml_weights = sem("ml_weights")
        ml_weighted = sem("ml_weighted")
        ml_out = sem("ml_out")
        head_kept = sem("head_kept")
        rope_made = sem("rope_made")
        decay_in = sem("decay_in")
        ret_scores = sem("ret_scores")
        ret_decayed = sem("ret_decayed")
        ret_out = sem("ret_out")
        head_root = sem("head_root")
        head_normed = sem("head_normed")
        gate_tanh = sem("gate_tanh")
        gate_made = sem("gate_made")
        head_gated = sem("head_gated")
        odd_in = sem("odd_in")
        dve_step = sem("dve_step")
        pool_step = sem("pool_step")
        final_g_in = sem("final_g_in")
        out_made = sem("out_made")
        out_stored = sem("out_stored")

        PARAMS = 8 * 16

        def odd_stage_free(n):
            former = {2: ("q", 3), 3: ("k", 3), 6: ("q", 7), 7: ("k", 7), 8: ("rope", 3), 9: ("rope", 7)}[n]
            return turn_of(O_TURNS, T_O, *former) + 1

        def ps_t_free(pe, odd, s):
            turns, base = (O_TURNS, T_O) if odd else (E_TURNS, T_E)
            n = base + sum(slot < s for slot, _, _ in turns)
            pe.wait_ge(turn_act, n)
            pe.wait_ge(turn_dve, n)
            pairs = 8 * odd + sum(a + 1 < s for a in (O_ATT if odd else E_ATT))
            wait(pe, probT_act, pairs)
            wait(pe, probT_dve, pairs)
            wait(pe, head_kept, 4 * odd + sum(a + 1 < s for a in (O_RET if odd else E_MLSTM)))

        def ps_t_settled(eng, odd, s):
            if s - 1 in (O_ATT if odd else E_ATT):
                eng.wait_ge(probs_turned, 8 * odd + (O_ATT if odd else E_ATT).index(s - 1) + 1)
            if not odd and s - 1 in E_MLSTM:
                eng.wait_ge(ml_out, E_MLSTM.index(s - 1) + 1)
            if odd and s - 1 in O_RET:
                eng.wait_ge(ret_out, O_RET.index(s - 1) + 1)

        def x_ready(eng, c0, n):
            eng.wait_ge(drained[(c0 + n - 1) % 2], drains_after(c0 + n - 1))

        block = ctx.enter_context(nc.Block())

        @block.sync
        def _(sp):
            def load(u, slot, rows, src):
                wait(sp, hi_made, 2 * (u - 3))
                wait(sp, lo_made, 2 * (u - 3))
                sp.dma_start(raw[:, slot, 0:rows, :], src).then_inc(raw_in[slot], 16)

            def unit_src(w, k0, rows, c0):
                return w[k0 * P:(k0 + rows) * P, c0].rearrange("(k p) c -> p k c", p=P)

            def in_units(u0, w, chunks):
                for n, c in enumerate(chunks):
                    for i in range(4):
                        load(u0 + 4 * n + i, i, 4, unit_src(w, 4 * i, 4, slice(c * CW, (c + 1) * CW)))

            def ffn_units(layer, u0, u1):
                with sp.Fori(0, FCH) as j:
                    for i in range(8):
                        w = (w_gate, w_up)[i // 4][layer]
                        load(u0 + i + j * 8, i % 4, 4, unit_src(w, 4 * (i % 4), 4, bass.ds(j * CW, CW)))
                with sp.Fori(0, NCH) as n:
                    for i, rows in enumerate(UNITS_DOWN):
                        load(u1 + i + n * 12, i % 4, rows,
                             unit_src(w_down[layer], STARTS_DOWN[i], rows, bass.ds(n * CW, CW)))

            sp.dma_start(ident[:], const[:, 0:P]).then_inc(first_in, 16)
            sp.dma_start(gain[:], gains).then_inc(first_in, 16)
            for n in range(NCH):
                cols = slice(n * CW, (n + 1) * CW)
                sp.dma_start(xs[:, :, cols], x[:, cols].rearrange("(t p) c -> p t c", p=P)).then_inc(x_in[n], 16)
                if n == 0:
                    load(0, 0, 4, unit_src(w_e, 0, 4, slice(2 * CW, 3 * CW)))
            for n, c in enumerate(E_ORDER):
                for i in range(4):
                    if n == 1 and i == 0:
                        sp.dma_start(gw[:], w_e[:, 9 * CW:EVEN_IN].rearrange("(k p) c -> p k c", p=P)).then_inc(params_in, 16)
                        sp.dma_start(upper[:], const[:, P:2 * P]).then_inc(params_in, 16)
                        sp.dma_start(win_f[:], const[:, 2 * P:2 * P + 512]).then_inc(params_in, 16)
                        sp.dma_start(sinkv[:], sinks.partition_broadcast(P)).then_inc(params_in, 16)
                        sp.dma_start(convp[:], conv).then_inc(params_in, 16)
                        sp.dma_start(gbias[:], gate_bias.partition_broadcast(P)).then_inc(params_in, 16)
                        sp.dma_start(selr[:], sel).then_inc(params_in, 16)
                        sp.dma_start(gnorm[:], b_norm_g.partition_broadcast(P)).then_inc(params_in, 16)
                    if n + i:
                        load(U_E + 4 * n + i, i, 4, unit_src(w_e, 4 * i, 4, slice(c * CW, (c + 1) * CW)))
            in_units(U_EO, w_eo, range(NCH))
            ffn_units(0, U_F0, U_D0)
            in_units(U_O, w_o, O_ORDER)
            in_units(U_OO, w_oo, range(NCH))
            ffn_units(1, U_F1, U_D1)
            sp.wait_ge(hi_made, 2 * (UNITS - 3))
            sp.wait_ge(lo_made, 2 * (UNITS - 3))
            sp.dma_start(raw[:, 0, :, :].rearrange("p k c -> p (k c)"),
                         final_g.partition_broadcast(P)).then_inc(final_g_in, 16)
            for t in range(TT):
                for h in range(2):
                    sp.wait_ge(out_made, 2 * t + h + 1)
                    cols = slice(h * 1024, (h + 1) * 1024)
                    sp.dma_start(out[t * P:(t + 1) * P, cols], xs[:, t, cols]).then_inc(out_stored, 16)
            sp.wait_ge(out_stored, 4 * 16)

        @block.scalar
        def _(act):
            def split_hi(h, j=0):
                rows, slot, r0 = half_rows(h), h // 2 % 4, 2 * (h % 2)
                act.wait_ge(raw_in[slot], 16 * (h // 8 + 1) + j * 32)
                wait(act, half_used, h - 3 + j * 16)
                act.activation(w_hi[:, h % 4, 0:rows, :], raw[:, slot, r0:r0 + rows, :],
                               ACT.Copy).then_inc(hi_made, 1)

            def turn_hi(t, src, dst, scale=None):
                act.wait_ge(turned, t + 1)
                if scale is None:
                    act.activation(dst, src, ACT.Copy).then_inc(turn_act, 1)
                else:
                    act.activation(dst, src, ACT.Identity, scale=scale).then_inc(turn_act, 1)

            def x_turn_hi(t, norm, kt):
                src = turn_psum(t)
                turn_hi(t, src, a_hi[:, kt, :].rearrange("p (t c) -> p t c", t=TT),
                        gain[:, norm, kt:kt + 1])

            def squares_of(norm, n, c0=None):
                if c0 is not None:
                    x_ready(act, c0, n + 1)
                for t in range(TT):
                    wait(act, squares, 8 * norm + 2 * n + t)
                    act.activation(junk[:], xs[:, t, n * CW:(n + 1) * CW], ACT.Square,
                                   accum_out=ssq[:, norm, t, n:n + 1]).then_inc(squares, 1)

            def root_of(norm):
                act.wait_ge(sum_made, norm + 1)
                act.activation(root[:, norm, :], ssum[:, norm, :], ACT.Sqrt, bias=eps[:, 0:1],
                               scale=1.0 / D).then_inc(root_made, 1)

            def attend_scores(k, gk):
                act.wait_ge(scores_made, gk + 1)
                act.wait_ge(max_made, gk + 1)
                wait(act, probs_turned, gk)
                for tt, (a, b) in enumerate(((0, 128), (128, 384))):
                    for hh in range(2):
                        act.activation(prob[:, hh, a:b], ps_s[:, hh, a:b], ACT.Exp,
                                       bias=nm[:, tt, hh:hh + 1],
                                       accum_out=psum_p[:, tt, hh:hh + 1]).then_inc(probs_made, 1)
                if gk < 8:
                    act.activation(es[:], sshift[:], ACT.Exp).then_inc(sinks_made, 1)

            def attend_turned(gk):
                act.wait_ge(probs_turned, gk + 1)
                wait(act, pv_made, gk)
                act.activation(probT[:, 0, :], ps_t[:, 0, 0:384], ACT.Copy).then_inc(probT_act, 1)

            def head_roots(n, heads):
                act.wait_ge(head_kept, n)
                act.activation(sd[:, heads, :], mv[:, heads, :, 1], ACT.Sqrt,
                               bias=eps[:, 0:1]).then_inc(head_root, 1)

            def even_drain(n):
                c = E_ORDER[n]
                pair = (C_E + n) % 2
                act.wait_ge(half_used, 2 * (U_E + 4 * n + 4))
                act.wait_ge(rstd_made, 1)
                ps = ps_g[:, pair, 0, :]
                r1, r8 = rstd[:, 0, 0, 0:1], rstd[:, 0, 1, 0:1]
                if c == 2:
                    for d in range(2):
                        act.activation(aknat[:, 0, :, d, :], ps[:, 0:256].rearrange("p (h d) -> p h d", d=64),
                                       ACT.Identity, scale=r1)
                    act.activation(av[:, 0, :], ps[:, 256:512], ACT.Identity,
                                   scale=r1).then_inc(drained[pair], 1)
                elif c in (0, 1):
                    act.activation(stage[:, n % 2, 0, :], ps, ACT.Identity, scale=r8).then_inc(drained[pair], 1)
                elif c in (3, 4):
                    act.wait_ge(turned, T_E + 4 + 4 * (n - 2))
                    act.activation(stage[:, n % 2, 0, :], ps, ACT.Identity, scale=r1).then_inc(drained[pair], 1)
                elif c in (5, 6):
                    h = 2 * (c - 5)
                    act.activation(mv_sb[:, 0, h:h + 2, 0:256], ps.rearrange("p (h d) -> p h d", h=2),
                                   ACT.Identity, scale=r1).then_inc(drained[pair], 1)
                else:
                    for t in range(TT):
                        act.activation(gfac[:, t, (c - 7) * CW:(c - 6) * CW], ps_g[:, pair, t, :], ACT.Tanh,
                                       scale=rstd[:, 0, 2, t:t + 1]).then_inc(drained[pair], 1)

            def even_side(s):
                for i, (slot, kind, b) in enumerate(E_TURNS):
                    if slot != s:
                        continue
                    t = T_E + i
                    src = turn_psum(t)
                    ps_t_settled(act, 0, s)
                    if kind == "y":
                        turn_hi(t, src, y_hi[:, b, :].rearrange("p (t c) -> p t c", t=TT))
                    elif kind == "conv":
                        wait(act, conv_made, b)
                        act.wait_ge(zeros_made, 3)
                        turn_hi(t, src[:, 0, :], cbuf[:, 3:3 + P])
                    else:
                        turn_hi(t, src[:, 0, :], (akT if kind == "k" else aqT)[:, b, 0:P])
                if s == 4:
                    act.wait_ge(gates_dve, 1)
                    act.activation(gsc[:, 1, :, :], gsc[:, 0, :, :], ACT.Exp).then_inc(gates_act, 1)
                if s == 5:
                    act.wait_ge(gates_dve, 2)
                    act.activation(gsc[:, 2, :, :], gsc[:, 1, :, :], ACT.Ln).then_inc(gates_act, 1)
                if s == 9:
                    act.wait_ge(gates_dve, 6)
                    act.activation(gsc[:, 7, :, :], gsc[:, 6, :, :], ACT.Exp, scale=-1.0).then_inc(gates_act, 1)
                if s in E_ATT:
                    attend_scores(E_ATT.index(s), E_ATT.index(s))
                if s - 1 in E_ATT:
                    attend_turned(E_ATT.index(s - 1))
                for b in range(8):
                    if s == 18 + 2 * b:
                        act.wait_ge(conv_made, b + 1)
                        wait(act, qk_made, b)
                        act.activation(cth[:], cacc[:, b % 2, :], ACT.Tanh, scale=0.5).then_inc(tanh_made, 1)
                if s in E_MLSTM:
                    h = E_MLSTM.index(s)
                    act.wait_ge(ml_scores, h + 1)
                    act.wait_ge(pair_made, 8)
                    wait(act, ml_weighted, h)
                    act.activation(wgt[:, 0:256], ps_s[:, 1, 0:256], ACT.Exp,
                                   bias=gsc[:, 4, 0, h:h + 1]).then_inc(ml_weights, 1)
                    act.activation(wgt[:, 256:384], ps_s[:, 1, 256:384], ACT.Exp,
                                   bias=gsc[:, 4, 1, h:h + 1]).then_inc(ml_weights, 1)
                if s < 36 and s % 4 == 3:
                    even_drain(s // 4)
                if s == 35:
                    head_roots(4, slice(0, 4))

            def odd_drain(n):
                c = O_ORDER[n]
                pair = (C_O + n) % 2
                act.wait_ge(half_used, 2 * (U_O + 4 * n + 4))
                act.wait_ge(rstd_made, 3)
                ps = ps_g[:, pair, 0, :]
                r1, r8 = rstd[:, 2, 0, 0:1], rstd[:, 2, 1, 0:1]
                if c < 4 or 6 <= c < 10:
                    if n in (2, 3, 6, 7, 8, 9):
                        act.wait_ge(turned, odd_stage_free(n))
                    act.activation(stage[:, n % 2, 0, :], ps, ACT.Identity,
                                   scale=r8 if c < 2 else r1).then_inc(drained[pair], 1)
                elif c < 6:
                    act.activation(cv[:, 0, (c - 4) * CW:(c - 3) * CW], ps, ACT.Identity,
                                   scale=r1).then_inc(drained[pair], 1)
                elif c < 12:
                    act.activation(rv[:, 0, (c - 10) * CW:(c - 9) * CW], ps, ACT.Identity,
                                   scale=r1).then_inc(drained[pair], 1)
                else:
                    for t in range(TT):
                        act.activation(gfac[:, t, (c - 12) * CW:(c - 11) * CW], ps_g[:, pair, t, :], ACT.Tanh,
                                       scale=rstd[:, 2, 2, t:t + 1]).then_inc(gate_tanh, 1)

            def load_bias(k):
                if k >= 2:
                    act.wait_ge(scores_made, 8 + k - 1)
                for hh in range(2):
                    src = bass.AP(rel.tensor, (2 * k + hh) * 383, [[1, P], [1, S]])
                    act.dma_start(biasT[:, k % 2, hh, :], src).then_inc(bias_in[k % 2], 16)

            def odd_side(s):
                for i, (slot, kind, b) in enumerate(O_TURNS):
                    if slot != s:
                        continue
                    t = T_O + i
                    src = turn_psum(t)
                    ps_t_settled(act, 1, s)
                    if kind == "y":
                        turn_hi(t, src, y_hi[:, b, :].rearrange("p (t c) -> p t c", t=TT))
                    elif kind == "rope":
                        g, h = b // 4, b % 4
                        turn_hi(t, src[:, 0, :], (rqT, rkT)[g % 2][:, 4 * (g // 2) + h, 0:P])
                    else:
                        turn_hi(t, src[:, 0, :], (cqT if kind == "q" else ckT)[:, b, 0:P])
                if s == 4:
                    load_bias(0)
                    load_bias(1)
                    act.dma_start(trig[:].rearrange("p a t c -> p (a t c)"),
                                  const[:, 768:1024]).then_inc(odd_in, 16)
                    act.dma_start(flip[:], const[:, 1024:1152]).then_inc(odd_in, 16)
                if s in O_ATT:
                    k = O_ATT.index(s)
                    attend_scores(k, 8 + k)
                    if k < 6:
                        load_bias(k + 2)
                    if k == 7:
                        act.dma_start(decay[:].rearrange("p h c -> p (h c)"), dtab).then_inc(decay_in, 16)
                if s - 1 in O_ATT:
                    attend_turned(8 + O_ATT.index(s - 1))
                if s == 44:
                    act.wait_ge(pv_made, 16)
                    act.dma_start(gnorm_o[:], d_norm_g.partition_broadcast(P)).then_inc(odd_in, 16)
                if s < 56 and s % 4 == 3:
                    odd_drain(s // 4)
                if s == 51:
                    head_roots(8, slice(0, 4))
                if s == 55:
                    head_roots(12, slice(4, 8))

            act.wait_ge(zeros_made, 1)
            act.wait_ge(first_in, 32)
            for b in range(8):
                x_turn_hi(T_X + b, 0, b)
                if b % 4 == 3:
                    split_hi(b // 4)
            split_hi(2)
            for s in range(36):
                split_ahead(split_hi, U_E + s)
                if s < 2:
                    for b in range(8 + 4 * s, 12 + 4 * s):
                        x_turn_hi(T_X + b, 0, b)
                    for n in (2 * s, 2 * s + 1):
                        act.wait_ge(x_in[n], 16)
                        squares_of(0, n)
                if s == 2:
                    root_of(0)
                if s == 3:
                    act.wait_ge(params_in, PARAMS)
                    act.activation(gw_hi[:], gw[:], ACT.Copy).then_inc(gatew_hi, 1)
                    act.activation(ident_b[:], ident[:], ACT.Copy).then_inc(consts_made, 1)
                    act.activation(win_b[:], win_f[:, 0:384], ACT.Copy).then_inc(consts_made, 1)
                    act.activation(tri_b[:], win_f[:, 384:512], ACT.Copy).then_inc(consts_made, 1)
                even_side(s)

            def out_proj(u0, side, late, t0, norm, cx):
                for n in range(NCH):
                    for i in range(4):
                        split_ahead(split_hi, u0 + 4 * n + i)
                        side(late + 4 * n + i)
                        if n >= 1:
                            x_turn_hi(t0 + 4 * (n - 1) + i, norm, 4 * (n - 1) + i)
                        if n >= 1 and i == 3:
                            squares_of(norm, n - 1, cx)

            def last_x(s, t0, norm, cx):
                if s < 2:
                    for b in (2 * s, 2 * s + 1):
                        x_turn_hi(t0 + 12 + b, norm, 12 + b)
                if s == 2:
                    squares_of(norm, NCH - 1, cx)
                    root_of(norm)

            def swiglu(u0, c0, t0, norm, tcx, cx, j):
                for i in range(8):
                    split_ahead(split_hi, u0 + i, j)
                    if isinstance(j, int):
                        last_x(i, tcx, norm, cx)
                    elif i < 4:
                        t = t0 + i + j * 4 - 4
                        act.wait_ge(turned, t + 1)
                        act.activation(h_hi[:, bass.ds(j * 4 + (i - 4), 1), :].rearrange("p a (t c) -> p (a t) c", t=TT),
                                       ring[region[t0 + i]], ACT.Copy).then_inc(turn_act, 1)
                    if i == 3:
                        act.wait_ge(half_used, 2 * (u0 + 4 + j * 8))
                        act.wait_ge(drained[(c0 + 1) % 2], 2 * ((c0 + 1) // 2) + j * 2)
                        act.wait_ge(rstd_made, norm + 1)
                        for t in range(TT):
                            act.activation(silu[:, t, :], ps_g[:, c0 % 2, t, :], ACT.Silu,
                                           scale=rstd[:, norm, 0, t:t + 1]).then_inc(drained[c0 % 2], 1)

            def down(u0, t0, tcx, norm, cx, n):
                for i in range(12):
                    split_ahead(split_hi, u0 + 12 * n + i)
                    if n == 0 and i < 4:
                        t = t0 + FKT - 4 + i
                        turn_hi(t, turn_psum(t), h_hi[:, FKT - 4 + i, :].rearrange("p (t c) -> p t c", t=TT))
                    if n >= 1 and i < 4 and tcx is not None:
                        x_turn_hi(tcx + 4 * (n - 1) + i, norm, 4 * (n - 1) + i)
                    if n >= 1 and i == 4:
                        squares_of(norm, n - 1, cx)

            out_proj(U_EO, even_side, 36, T_EO, 1, C_EO)
            swiglu(U_F0, C_F0, T_F0, 1, T_EO, C_EO, 0)
            with act.Fori(1, FCH) as j:
                swiglu(U_F0, C_F0, T_F0, 1, T_EO, C_EO, j)
            for n in range(NCH):
                down(U_D0, T_F0, T_D0, 2, C_D0, n)
            for s in range(56):
                split_ahead(split_hi, U_O + s)
                last_x(s, T_D0, 2, C_D0)
                odd_side(s)
            out_proj(U_OO, odd_side, 56, T_OO, 3, C_OO)
            swiglu(U_F1, C_F1, T_F1, 3, T_OO, C_OO, 0)
            with act.Fori(1, FCH) as j:
                swiglu(U_F1, C_F1, T_F1, 3, T_OO, C_OO, j)
            for n in range(NCH):
                down(U_D1, T_F1, None, 4, C_D1, n)
            squares_of(4, NCH - 1, C_D1)
            root_of(4)

        @block.vector
        def _(dve):
            steps = [0]

            def link(ins):
                steps[0] += 1
                ins.then_inc(dve_step, 1)
                dve.wait_ge(dve_step, steps[0])

            def split_lo(h, j=0):
                rows, slot, r0 = half_rows(h), h // 2 % 4, 2 * (h % 2)
                dve.wait_ge(hi_made, h + 1 + j * 16)
                wait(dve, half_used, h - 3 + j * 16)
                dve.tensor_tensor(w_lo[:, h % 4, 0:rows, :], raw[:, slot, r0:r0 + rows, :],
                                  w_hi[:, h % 4, 0:rows, :].bitcast(F32), ALU.subtract).then_inc(lo_made, 1)

            def turn_lo(t, src, hi, lo):
                dve.wait_ge(turn_act, t + 1)
                dve.tensor_tensor(lo.rearrange("p (t c) -> p t c", t=TT), src,
                                  hi.bitcast(F32).rearrange("p (t c) -> p t c", t=TT),
                                  ALU.subtract).then_inc(turn_dve, 1)

            def x_turn_lo(t, norm, kt):
                dve.wait_ge(turn_act, t + 1)
                dve.scalar_tensor_tensor(a_lo[:, kt, :].rearrange("p (t c) -> p t c", t=TT), turn_psum(t),
                                         gain[:, norm, kt:kt + 1],
                                         a_hi[:, kt, :].bitcast(F32).rearrange("p (t c) -> p t c", t=TT),
                                         ALU.mult, ALU.subtract).then_inc(turn_dve, 1)

            def turn_copy(t, src, dst):
                dve.wait_ge(turned, t + 1)
                dve.tensor_copy(dst, src).then_inc(turn_dve, 1)

            def rstd_of(norm):
                dve.wait_ge(squares, 8 * norm + 8)
                dve.tensor_reduce(ssum[:, norm, :], ssq[:, norm, :, :], AX.X, ALU.add).then_inc(sum_made, 1)
                dve.wait_ge(root_made, norm + 1)
                link(dve.reciprocal(rstd[:, norm, 0, :], root[:, norm, :]))
                link(dve.tensor_scalar(rstd[:, norm, 1, :], rstd[:, norm, 0, :], 0.125, None, ALU.mult))
                dve.tensor_scalar(rstd[:, norm, 2, :], rstd[:, norm, 0, :], 0.5, None,
                                  ALU.mult).then_inc(rstd_made, 1)

            def attend_max(k, gk):
                dve.wait_ge(scores_made, gk + 1)
                wait(dve, probs_made, 4 * gk)
                link(dve.tensor_reduce(mx[:, 0, :], ps_s[:, :, 0:128], AX.X, ALU.max))
                link(dve.tensor_reduce(mx[:, 1, :], ps_s[:, :, 128:384], AX.X, ALU.max))
                if gk < 8:
                    wait(dve, sinks_made, gk)
                    link(dve.scalar_tensor_tensor(nm[:], mx[:], -1.0, nsink[:, k, :, :], ALU.mult, ALU.min))
                    dve.tensor_tensor(sshift[:], nm[:], sinkv[:, k, :, :], ALU.add).then_inc(max_made, 1)
                else:
                    dve.tensor_scalar(nm[:], mx[:], -1.0, None, ALU.mult).then_inc(max_made, 1)

            def attend_turned(gk):
                dve.wait_ge(probs_turned, gk + 1)
                wait(dve, pv_made, gk)
                dve.tensor_copy(probT[:, 1, :], ps_t[:, 1, 0:384]).then_inc(probT_dve, 1)
                dve.wait_ge(probs_made, 4 * gk + 4)
                if gk < 8:
                    dve.wait_ge(sinks_made, gk + 1)
                    link(dve.tensor_tensor(den[:], psum_p[:], es[:], ALU.add))
                    link(dve.reciprocal(rden[:], den[:]))
                else:
                    link(dve.reciprocal(rden[:], psum_p[:]))

            def attend_out(gk, former_turn):
                dve.wait_ge(pv_made, gk + 1)
                if gk < 7:
                    dve.wait_ge(scores_made, gk + 2)
                if gk == 7:
                    dve.wait_ge(ml_scores, 1)
                wait(dve, turned, former_turn + 1)
                dve.tensor_tensor(yp[:].rearrange("p t (h d) -> p t h d", h=2),
                                  ps_s[:, :, 384:512].rearrange("p t (h d) -> p t h d", h=2),
                                  rden[:].unsqueeze(3).to_broadcast([P, 2, 2, 64]),
                                  ALU.mult).then_inc(pair_made, 1)

            def head_norm(n, heads, y):
                dve.wait_ge(head_root, n)
                link(dve.reciprocal(rs[:, heads, :], sd[:, heads, :]))
                for h in range(heads.start, heads.stop):
                    for t in range(TT):
                        ins = dve.tensor_scalar(y[:, t, h, :], y[:, t, h, :], mv[:, h, t, 0:1],
                                                rs[:, h, t:t + 1], ALU.subtract, ALU.mult)
                    ins.then_inc(head_normed, 1)

            def even_drain(n):
                c = E_ORDER[n]
                pair = (C_E + n) % 2
                if c >= 7:
                    return
                dve.wait_ge(half_used, 2 * (U_E + 4 * n + 4))
                dve.wait_ge(rstd_made, 1)
                ps = ps_g[:, pair, 1, :]
                r1, r8 = rstd[:, 0, 0, 1:2], rstd[:, 0, 1, 1:2]
                if c == 2:
                    for d in range(2):
                        dve.tensor_scalar(aknat[:, 1, :, d, :], ps[:, 0:256].rearrange("p (h d) -> p h d", d=64),
                                          r1, None, ALU.mult)
                    dve.tensor_scalar(av[:, 1, :], ps[:, 256:512], r1, None, ALU.mult).then_inc(drained[pair], 1)
                elif c in (0, 1):
                    dve.tensor_scalar(stage[:, n % 2, 1, :], ps, r8, None, ALU.mult).then_inc(drained[pair], 1)
                elif c in (3, 4):
                    dve.wait_ge(turned, T_E + 4 + 4 * (n - 2))
                    dve.tensor_scalar(stage[:, n % 2, 1, :], ps, r1, None, ALU.mult).then_inc(drained[pair], 1)
                else:
                    h = 2 * (c - 5)
                    dve.tensor_scalar(mv_sb[:, 1, h:h + 2, 0:256], ps.rearrange("p (h d) -> p h d", h=2),
                                      r1, None, ALU.mult).then_inc(drained[pair], 1)

            def convolve(b):
                dve.wait_ge(turn_act, turn_of(E_TURNS, T_E, "conv", b) + 1)
                dve.wait_ge(turn_dve, turn_of(E_TURNS, T_E, "conv", b) + 1)
                acc = cacc[:, b % 2, :]
                link(dve.tensor_scalar(acc, cbuf[:, 3:3 + S], convp[:, b, 3:4], convp[:, b, 4:5],
                                       ALU.mult, ALU.add))
                for j in (2, 1):
                    link(dve.scalar_tensor_tensor(acc, cbuf[:, j:j + S], convp[:, b, j:j + 1], acc,
                                                  ALU.mult, ALU.add))
                dve.scalar_tensor_tensor(acc, cbuf[:, 0:S], convp[:, b, 0:1], acc,
                                         ALU.mult, ALU.add).then_inc(conv_made, 1)

            def gates(s):
                if s == 4:
                    dve.wait_ge(gates_mm, 1)
                    for t in range(TT):
                        ins = dve.scalar_tensor_tensor(gx[:, t, :], ps_s[:, 0, 8 * t:8 * t + 8],
                                                       rstd[:, 0, 0, t:t + 1], gbias[:], ALU.mult, ALU.add)
                        link(ins)
                    dve.scalar_tensor_tensor(gsc[:, 0, :, :], gx[:, :, 4:8], -1.0, gx[:, :, 4:8],
                                             ALU.mult, ALU.min).then_inc(gates_dve, 1)
                if s == 5:
                    dve.wait_ge(gates_act, 1)
                    dve.tensor_scalar(gsc[:, 1, :, :], gsc[:, 1, :, :], 1.0, None,
                                      ALU.add).then_inc(gates_dve, 1)
                if s == 6:
                    dve.wait_ge(gates_act, 2)
                    dve.scalar_tensor_tensor(gsc[:, 3, :, :], gx[:, :, 4:8], 0.0, gsc[:, 2, :, :],
                                             ALU.min, ALU.subtract).then_inc(gates_dve, 1)
                if s == 7:
                    dve.wait_ge(gates_mm, 2)
                    fsum = ps_s[:, 0, 16:24].rearrange("p (t h) -> p t h", t=TT)
                    link(dve.tensor_copy(gsc[:, 5, :, :], fsum))
                    dve.tensor_tensor(gsc[:, 4, :, :], gx[:, :, 0:4], gsc[:, 5, :, :],
                                      ALU.subtract).then_inc(gates_dve, 1)
                if s == 8:
                    dve.wait_ge(gates_mm, 3)
                    dve.wait_ge(zeros_made, 3)
                    link(dve.tensor_copy(cmax[:, 0, P:P + S], ps_s[0:4, 1, 0:S]))
                    link(dve.tensor_scalar(cmax[:, 0, P:P + S], cmax[:, 0, P:P + S], 0.0, None, ALU.max))
                    for j in range(8):
                        a, b, d = j % 2, 1 - j % 2, 1 << j
                        link(dve.tensor_tensor(cmax[:, b, P:P + S], cmax[:, a, P:P + S],
                                               cmax[:, a, P - d:P - d + S], ALU.max))
                    dve.tensor_scalar(negm[:], cmax[:, 0, P:P + S], -1.0, None, ALU.mult).then_inc(gates_dve, 1)
                if s == 9:
                    dve.wait_ge(gates_mm, 4)
                    mnat = ps_s[:, 0, 32:40].rearrange("p (t h) -> p t h", t=TT)
                    dve.tensor_tensor(gsc[:, 6, :, :], gsc[:, 5, :, :], mnat, ALU.add).then_inc(gates_dve, 1)

            def mlstm_out(h):
                dve.wait_ge(ml_out, h + 1)
                link(dve.tensor_copy(den[:, 0, :].unsqueeze(2), ps_t[:, :, 256:257]))
                link(dve.scalar_tensor_tensor(den[:, 1, :], den[:, 0, :], -1.0, den[:, 0, :], ALU.mult, ALU.max))
                link(dve.tensor_tensor(den[:, 0, :], den[:, 1, :], gsc[:, 7, :, h], ALU.max))
                link(dve.reciprocal(rden[:, 0, :], den[:, 0, :]))
                for t in range(TT):
                    ins = dve.tensor_scalar(yB[:, t, h, :], ps_t[:, t, 0:256], rden[:, 0, t:t + 1], None, ALU.mult)
                link(ins)
                for t in range(TT):
                    ins = dve.bn_stats(stats[:, h, t, :], yB[:, t, h, :])
                link(ins)
                for t in range(TT):
                    ins = dve.bn_aggr(mv[:, h, t, :], stats[:, h, t, :])
                ins.then_inc(head_kept, 1)

            def even_side(s):
                if s == 4 or s in (5, 6, 7, 8, 9):
                    gates(s)
                if s - 2 in E_ATT:
                    k = E_ATT.index(s - 2)
                    attend_out(k, turn_of(E_TURNS, T_E, "y", k - 1) if k else -1)
                if s in E_ATT:
                    attend_max(E_ATT.index(s), E_ATT.index(s))
                for i, (slot, kind, b) in enumerate(E_TURNS):
                    if slot != s:
                        continue
                    t = T_E + i
                    src = turn_psum(t)
                    ps_t_settled(dve, 0, s)
                    if kind == "y":
                        if s - 1 in E_ATT:
                            dve.wait_ge(probT_act, E_ATT.index(s - 1) + 1)
                        turn_lo(t, src, y_hi[:, b, :], y_lo[:, b, :])
                    elif kind == "conv":
                        turn_copy(t, src[:, 1, :], cbuf[:, 3 + P:3 + S])
                        convolve(b)
                    else:
                        turn_copy(t, src[:, 1, :], (akT if kind == "k" else aqT)[:, b, P:S])
                if s - 1 in E_ATT:
                    attend_turned(E_ATT.index(s - 1))
                for b in range(8):
                    if s == 18 + 2 * b:
                        dve.wait_ge(tanh_made, b + 1)
                        dve.scalar_tensor_tensor(mqk[:, b, :], cth[:], 1.0, cacc[:, b % 2, :],
                                                 ALU.add, ALU.mult).then_inc(qk_made, 1)
                if s in E_MLSTM:
                    h = E_MLSTM.index(s)
                    dve.wait_ge(ml_weights, 2 * h + 2)
                    wait(dve, ml_out, h)
                    dve.scalar_tensor_tensor(scT[:], ps_s[:, 0, 0:384], MLSTM_SCALE, wgt[:],
                                             ALU.mult, ALU.mult).then_inc(ml_weighted, 1)
                if s - 1 in E_MLSTM:
                    mlstm_out(E_MLSTM.index(s - 1))
                if s < 36 and s % 4 == 3:
                    even_drain(s // 4)
                if s == 35:
                    head_norm(1, slice(0, 4), yB)

            def odd_drain(n):
                c = O_ORDER[n]
                pair = (C_O + n) % 2
                dve.wait_ge(half_used, 2 * (U_O + 4 * n + 4))
                dve.wait_ge(rstd_made, 3)
                ps = ps_g[:, pair, 1, :]
                r1, r8 = rstd[:, 2, 0, 1:2], rstd[:, 2, 1, 1:2]
                if c < 4 or 6 <= c < 10:
                    if n in (2, 3, 6, 7, 8, 9):
                        dve.wait_ge(turned, odd_stage_free(n))
                    dve.tensor_scalar(stage[:, n % 2, 1, :], ps, r8 if c < 2 else r1, None,
                                      ALU.mult).then_inc(drained[pair], 1)
                elif c < 6:
                    dve.tensor_scalar(cv[:, 1, (c - 4) * CW:(c - 3) * CW], ps, r1, None,
                                      ALU.mult).then_inc(drained[pair], 1)
                elif c < 12:
                    dve.tensor_scalar(rv[:, 1, (c - 10) * CW:(c - 9) * CW], ps, r1, None,
                                      ALU.mult).then_inc(drained[pair], 1)
                else:
                    dve.wait_ge(gate_tanh, 2 * (c - 12) + 2)
                    dve.wait_ge(turned, turn_of(O_TURNS, T_O, "rope", (11, 15)[c - 12]) + 1)
                    for t in range(TT):
                        dve.tensor_scalar(stage[:, n % 2, t, :], ps_g[:, pair, t, :], rstd[:, 2, 0, t:t + 1],
                                          None, ALU.mult).then_inc(drained[pair], 1)

            def odd_side(s):
                if s in O_ATT:
                    attend_max(O_ATT.index(s), 8 + O_ATT.index(s))
                for i, (slot, kind, b) in enumerate(O_TURNS):
                    if slot != s:
                        continue
                    t = T_O + i
                    src = turn_psum(t)
                    ps_t_settled(dve, 1, s)
                    if kind == "y":
                        turn_lo(t, src, y_hi[:, b, :], y_lo[:, b, :])
                    elif kind == "rope":
                        g, h = b // 4, b % 4
                        turn_copy(t, src[:, 1, :], (rqT, rkT)[g % 2][:, 4 * (g // 2) + h, P:S])
                    else:
                        turn_copy(t, src[:, 1, :], (cqT if kind == "q" else ckT)[:, b, P:S])
                if s - 1 in O_ATT:
                    attend_turned(8 + O_ATT.index(s - 1))
                if s - 2 in O_ATT:
                    k = O_ATT.index(s - 2)
                    attend_out(8 + k, turn_of(O_TURNS, T_O, "y", k - 1) if k else -1)
                if s in O_RET:
                    h = O_RET.index(s)
                    dve.wait_ge(decay_in, 16)
                    dve.wait_ge(ret_scores, h + 1)
                    wait(dve, ret_out, h - 1)
                    sc = scD[:, h % 2, :]
                    dve.tensor_tensor(sc[:, 0:256], ps_s[:, h % 2, 0:256], decay[:, h, :], ALU.mult)
                    dve.tensor_tensor(sc[:, 256:384], ps_s[:, h % 2, 256:384], decay[:, h, 0:128],
                                      ALU.mult).then_inc(ret_decayed, 1)
                if s - 1 in O_RET:
                    h = O_RET.index(s - 1)
                    dve.wait_ge(ret_out, h + 1)
                    dve.wait_ge(turn_act, T_O + sum(slot <= s for slot, _, _ in O_TURNS))
                    link(dve.tensor_copy(yD[:, :, h, :], ps_t[:, h % 2, 0:256].rearrange("p (t c) -> p t c", t=TT)))
                    for t in range(TT):
                        ins = dve.bn_stats(stats[:, h, t, :], yD[:, t, h, :])
                    link(ins)
                    for t in range(TT):
                        ins = dve.bn_aggr(mv[:, h, t, :], stats[:, h, t, :])
                    ins.then_inc(head_kept, 1)
                if s < 56 and s % 4 == 3:
                    odd_drain(s // 4)
                if s == 51:
                    head_norm(2, slice(0, 4), yD)
                if s == 55:
                    head_norm(3, slice(4, 8), yD)

            dve.memset(eps[:], EPS).then_inc(zeros_made, 1)
            dve.memset(cbuf[:, 0:3], 0.0).then_inc(zeros_made, 1)
            dve.memset(cmax[:, :, 0:P], 0.0).then_inc(zeros_made, 1)
            dve.memset(mv_sb[:, :, :, 256:257], 1.0).then_inc(zeros_made, 1)
            dve.memset(ones[:], 1.0).then_inc(zeros_made, 1)
            dve.wait_ge(first_in, 32)
            for b in range(8):
                x_turn_lo(T_X + b, 0, b)
                if b % 4 == 3:
                    split_lo(b // 4)
            split_lo(2)
            for s in range(36):
                split_ahead(split_lo, U_E + s)
                if s < 2:
                    for b in range(8 + 4 * s, 12 + 4 * s):
                        x_turn_lo(T_X + b, 0, b)
                if s == 3:
                    dve.wait_ge(params_in, PARAMS)
                    dve.tensor_scalar(nsink[:], sinkv[:], -1.0, None, ALU.mult).then_inc(zeros_made, 1)
                    dve.wait_ge(gatew_hi, 1)
                    dve.tensor_tensor(gw_lo[:], gw[:], gw_hi[:].bitcast(F32), ALU.subtract).then_inc(gatew_lo, 1)
                if s == 2:
                    rstd_of(0)
                even_side(s)

            def add_x(u_end, pair, n):
                dve.wait_ge(half_used, 2 * (u_end))
                for t in range(TT):
                    cols = xs[:, t, n * CW:(n + 1) * CW]
                    dve.tensor_tensor(cols, ps_g[:, pair, t, :], cols, ALU.add).then_inc(drained[pair], 1)

            def out_proj(u0, c0, side, late, t0, norm):
                for n in range(NCH):
                    for i in range(4):
                        split_ahead(split_lo, u0 + 4 * n + i)
                        side(late + 4 * n + i)
                        if n >= 1:
                            x_turn_lo(t0 + 4 * (n - 1) + i, norm, 4 * (n - 1) + i)
                    add_x(u0 + 4 * n + 4, (c0 + n) % 2, n)

            def last_x(s, t0, norm):
                if s < 2:
                    for b in (2 * s, 2 * s + 1):
                        x_turn_lo(t0 + 12 + b, norm, 12 + b)
                if s == 2:
                    rstd_of(norm)

            def swiglu(u0, c0, t0, norm, tcx, j):
                for i in range(8):
                    split_ahead(split_lo, u0 + i, j)
                    if isinstance(j, int):
                        last_x(i, tcx, norm)
                    elif i < 4:
                        t = t0 + i + j * 4 - 4
                        dve.wait_ge(turn_act, t + 1)
                        kt = bass.ds(j * 4 + (i - 4), 1)
                        dve.tensor_tensor(h_lo[:, kt, :].rearrange("p a (t c) -> p (a t) c", t=TT),
                                          ring[region[t0 + i]],
                                          h_hi[:, kt, :].bitcast(F32).rearrange("p a (t c) -> p (a t) c", t=TT),
                                          ALU.subtract).then_inc(turn_dve, 1)
                    if i == 7:
                        dve.wait_ge(half_used, 2 * (u0 + 8 + j * 8))
                        dve.wait_ge(rstd_made, norm + 1)
                        dve.wait_ge(drained[c0 % 2], 2 * (c0 // 2) + 2 + j * 2)
                        for t in range(TT):
                            dve.scalar_tensor_tensor(prod[:, t, :], ps_g[:, (c0 + 1) % 2, t, :],
                                                     rstd[:, norm, 0, t:t + 1], silu[:, t, :],
                                                     ALU.mult, ALU.mult).then_inc(drained[(c0 + 1) % 2], 1)

            def down(u0, c0, t0, tcx, norm, n):
                for i in range(12):
                    split_ahead(split_lo, u0 + 12 * n + i)
                    if n == 0 and i < 4:
                        t = t0 + FKT - 4 + i
                        turn_lo(t, turn_psum(t), h_hi[:, FKT - 4 + i, :], h_lo[:, FKT - 4 + i, :])
                    if n >= 1 and i < 4 and tcx is not None:
                        x_turn_lo(tcx + 4 * (n - 1) + i, norm, 4 * (n - 1) + i)
                add_x(u0 + 12 * n + 12, (c0 + n) % 2, n)

            out_proj(U_EO, C_EO, even_side, 36, T_EO, 1)
            swiglu(U_F0, C_F0, T_F0, 1, T_EO, 0)
            with dve.Fori(1, FCH) as j:
                swiglu(U_F0, C_F0, T_F0, 1, T_EO, j)
            for n in range(NCH):
                down(U_D0, C_D0, T_F0, T_D0, 2, n)
            for s in range(56):
                split_ahead(split_lo, U_O + s)
                last_x(s, T_D0, 2)
                odd_side(s)
            out_proj(U_OO, C_OO, odd_side, 56, T_OO, 3)
            swiglu(U_F1, C_F1, T_F1, 3, T_OO, 0)
            with dve.Fori(1, FCH) as j:
                swiglu(U_F1, C_F1, T_F1, 3, T_OO, j)
            for n in range(NCH):
                down(U_D1, C_D1, T_F1, None, 4, n)
            rstd_of(4)
            dve.wait_ge(rstd_made, 5)
            dve.wait_ge(final_g_in, 16)
            g = raw[:, 0, :, :].rearrange("p k c -> p (k c)")
            for t in range(TT):
                for h in range(2):
                    cols = slice(h * 1024, (h + 1) * 1024)
                    dve.scalar_tensor_tensor(xs[:, t, cols], xs[:, t, cols], rstd[:, 4, 0, t:t + 1], g[:, cols],
                                             ALU.mult, ALU.mult).then_inc(out_made, 1)

        @block.gpsimd
        def _(pool):
            steps = [0]

            def link(ins):
                steps[0] += 1
                ins.then_inc(pool_step, 1)
                pool.wait_ge(pool_step, steps[0])

            def gate_factor(cols, g, x=None):
                link(pool.tensor_scalar(gfac[:, :, cols], gfac[:, :, cols], 1.0, 0.5, ALU.add, ALU.mult))
                if x is not None:
                    link(pool.tensor_tensor(gfac[:, :, cols], gfac[:, :, cols], x, ALU.mult))
                for t in range(TT):
                    ins = pool.tensor_tensor(gfac[:, t, cols], gfac[:, t, cols], g[:, cols], ALU.mult)
                ins.then_inc(gate_made, 1)

            def gated(n, gates, y, h, width):
                pool.wait_ge(head_normed, n + 1)
                pool.wait_ge(gate_made, gates)
                pool.tensor_tensor(y[:, :, h, :], y[:, :, h, :], gfac[:, :, h * width:(h + 1) * width],
                                   ALU.mult).then_inc(head_gated, 1)

            pool.wait_ge(params_in, PARAMS)
            for c in range(2):
                n = 7 + c
                pool.wait_ge(drained[(C_E + n) % 2], 2 * ((C_E + n) // 2) + 2)
                gate_factor(slice(c * CW, (c + 1) * CW), gnorm[:])
            for h in range(4):
                gated(h, h // 2 + 1, yB, h, 256)
            pool.wait_ge(odd_in, 32)
            for k in range(2):
                pool.wait_ge(bias_in[k % 2], 32 * (k // 2) + 32)
                pool.memset(biasT[0:64, k % 2, :, 0:64], NEG).then_inc(bias_masked, 1)

            def rope(r, n):
                pool.wait_ge(drained[(C_O + n) % 2], 2 * ((C_O + n) // 2) + 2)
                for t in range(TT):
                    x = stage[:, n % 2, t, :].rearrange("p (h a d) -> p h a d", h=4, a=2)
                    x1, x2 = x[:, :, 0, :], x[:, :, 1, :]
                    cos = trig[:, 0, t, :].unsqueeze(1).to_broadcast([P, 4, 64])
                    sin = trig[:, 1, t, :].unsqueeze(1).to_broadcast([P, 4, 64])
                    pool.tensor_tensor(rtmp[:, 0, t, :, :], x1, sin, ALU.mult)
                    link(pool.tensor_tensor(rtmp[:, 1, t, :, :], x2, sin, ALU.mult))
                    pool.tensor_tensor(x1, x1, cos, ALU.mult)
                    link(pool.tensor_tensor(x2, x2, cos, ALU.mult))
                    pool.tensor_tensor(x1, x1, rtmp[:, 1, t, :, :], ALU.subtract)
                    ins = pool.tensor_tensor(x2, x2, rtmp[:, 0, t, :, :], ALU.add)
                    if t == 0:
                        link(ins)
                ins.then_inc(rope_made, 1)

            for k in range(2, 8):
                pool.wait_ge(bias_in[k % 2], 32 * (k // 2) + 32)
                pool.memset(biasT[0:64, k % 2, :, 0:64], NEG).then_inc(bias_masked, 1)
                if k in (4, 5, 6, 7):
                    rope(k - 4, k + 2)
            for c in range(2):
                n = 12 + c
                pool.wait_ge(drained[(C_O + n) % 2], 2 * ((C_O + n) // 2) + 2)
                pool.wait_ge(odd_in, 48)
                cols = slice(c * CW, (c + 1) * CW)
                gate_factor(cols, gnorm_o[:], stage[:, n % 2, :, :])
                for h in range(4 * c, 4 * c + 4):
                    gated(4 + h, 3 + c, yD, h, 128)

        @block.tensor
        def _(pe):
            def unit(u, k0, pair, hi, lo, first, last, j=0):
                for h in (2 * u, 2 * u + 1):
                    pe.wait_ge(hi_made, h + 1 + j * 16)
                    pe.wait_ge(lo_made, h + 1 + j * 16)
                    for k in range(half_rows(h)):
                        kt = k0 + 2 * (h % 2) + k
                        end = last and kt == k0 + UNIT_ROWS[u] - 1
                        for t in range(TT):
                            tok = slice(t * P, (t + 1) * P)
                            acc = ps_g[:, pair, t, :]
                            wh, wl = w_hi[:, h % 4, k, :], w_lo[:, h % 4, k, :]
                            pe.matmul(acc, hi[:, kt, tok], wh, start=first and kt == k0, stop=False)
                            pe.matmul(acc, hi[:, kt, tok], wl, start=False, stop=False)
                            ins = pe.matmul(acc, lo[:, kt, tok], wh, start=False, stop=end)
                    ins.then_inc(half_used, 1)

            def chunk_free(chunk):
                wait(pe, drained[chunk % 2], drains_before(chunk))

            def turn(t, src0, src1):
                before = turn_before(t)
                wait(pe, turn_act, before + 1)
                wait(pe, turn_dve, before + 1)
                dst = turn_psum(t)
                pe.transpose(dst[:, 0, :], src0, ident[:])
                pe.transpose(dst[:, 1, :], src1, ident[:]).then_inc(turned, 1)

            def x_turn(t, kt):
                cols = slice(kt * P, (kt + 1) * P)
                turn(t, xs[:, 0, cols], xs[:, 1, cols])

            def operand_ready(t):
                pe.wait_ge(turn_act, t + 1)
                pe.wait_ge(turn_dve, t + 1)

            def attend_pv(gk, v):
                pe.wait_ge(probT_act, gk + 1)
                pe.wait_ge(probT_dve, gk + 1)
                wait(pe, pair_made, gk)
                for hh in range(2):
                    o = slice(384 + 64 * hh, 448 + 64 * hh)
                    pe.matmul(ps_s[:, 0, o], probT[:, hh, 0:128], v(0, hh), start=True, stop=True)
                    pe.matmul(ps_s[:, 1, o], probT[:, hh, 128:256], v(0, hh), start=True, stop=False)
                    ins = pe.matmul(ps_s[:, 1, o], probT[:, hh, 256:384], v(1, hh), start=False, stop=True)
                ins.then_inc(pv_made, 1)

            def attend_turn(gk):
                pe.wait_ge(probs_made, 4 * gk + 4)
                wait(pe, probT_act, gk)
                wait(pe, probT_dve, gk)
                for hh in range(2):
                    for b in range(3):
                        cols = slice(b * P, (b + 1) * P)
                        ins = pe.transpose(ps_t[:, hh, cols], prob[:, hh, cols], ident[:])
                ins.then_inc(probs_turned, 1)

            def even_scores(k):
                wait(pe, probs_made, 4 * k)
                pe.wait_ge(consts_made, 3)
                pe.wait_ge(gates_dve, 6)
                operand_ready(turn_of(E_TURNS, T_E, "q", k))
                kv = k // 2
                for hh in range(2):
                    half = slice(64 * hh, 64 * hh + 64)
                    s = ps_s[:, hh, :]
                    pe.matmul(s[:, 0:128], ident_b[:], win_b[:, 0:128], start=True, stop=False)
                    pe.matmul(s[:, 0:128], aqT[half, k, 0:P], akT[half, kv, 0:P], start=False, stop=True)
                    pe.matmul(s[:, 128:384], ident_b[:], win_b[:, 128:384], start=True, stop=False)
                    ins = pe.matmul(s[:, 128:384], aqT[half, k, P:S], akT[half, kv, :], start=False, stop=True)
                ins.then_inc(scores_made, 1)

            def gates(s):
                if s == 4:
                    pe.wait_ge(gatew_lo, 1)
                    for t in range(TT):
                        tok, o = slice(t * P, (t + 1) * P), ps_s[:, 0, 8 * t:8 * t + 8]
                        for k in range(KT):
                            pe.matmul(o, a_hi[:, k, tok], gw_hi[:, k, :], start=k == 0, stop=False)
                            pe.matmul(o, a_hi[:, k, tok], gw_lo[:, k, :], start=False, stop=False)
                            ins = pe.matmul(o, a_lo[:, k, tok], gw_hi[:, k, :], start=False, stop=k == KT - 1)
                    ins.then_inc(gates_mm, 1)
                if s == 7:
                    pe.wait_ge(gates_dve, 3)
                    pe.wait_ge(zeros_made, 5)
                    pe.matmul(ps_s[:, 0, 16:20], upper[:], gsc[:, 3, 0, :], start=True, stop=True)
                    pe.matmul(ps_s[:, 0, 20:24], ones[:], gsc[:, 3, 0, :], start=True, stop=False)
                    pe.matmul(ps_s[:, 0, 20:24], upper[:], gsc[:, 3, 1, :], start=False,
                              stop=True).then_inc(gates_mm, 1)
                if s == 8:
                    pe.wait_ge(gates_dve, 4)
                    pe.transpose(ps_s[0:4, 1, 0:P], gsc[:, 4, 0, :], ident[:])
                    pe.transpose(ps_s[0:4, 1, P:S], gsc[:, 4, 1, :], ident[:]).then_inc(gates_mm, 1)
                if s == 9:
                    pe.wait_ge(gates_dve, 5)
                    for t in range(TT):
                        ins = pe.transpose(ps_s[:, 0, 32 + 4 * t:36 + 4 * t],
                                           cmax[:, 0, P + t * P:P + (t + 1) * P], ident[0:4, 0:4])
                    ins.then_inc(gates_mm, 1)

            def mlstm_scores(h):
                pe.wait_ge(qk_made, 5 + h)
                pe.wait_ge(gates_act, 3)
                wait(pe, probs_made, 32)
                pe.wait_ge(pair_made, 8 if h else 7)
                wait(pe, ml_weighted, h)
                q, kk = mqk[:, h, :], mqk[:, 4 + h, :]
                pe.matmul(ps_s[:, 0, 0:256], kk[:, 0:P], q, start=True, stop=True)
                pe.matmul(ps_s[:, 0, 256:384], kk[:, P:S], q[:, P:S], start=True, stop=True)
                pe.matmul(ps_s[:, 1, 0:128], selr[:, h, :], negm[:, 0:P], start=True, stop=False)
                pe.matmul(ps_s[:, 1, 0:128], ident_b[:], tri_b[:], start=False, stop=True)
                pe.matmul(ps_s[:, 1, 128:256], selr[:, h, :], negm[:, P:S], start=True, stop=True)
                pe.matmul(ps_s[:, 1, 256:384], selr[:, h, :], negm[:, P:S], start=True, stop=False)
                pe.matmul(ps_s[:, 1, 256:384], ident_b[:], tri_b[:], start=False,
                          stop=True).then_inc(ml_scores, 1)

            def mlstm_values(h):
                pe.wait_ge(ml_weighted, h + 1)
                pe.wait_ge(zeros_made, 4)
                pe.wait_ge(drained[(5 + h // 2) % 2], drains_after(5 + h // 2))
                wait(pe, probT_act, 8)
                wait(pe, probT_dve, 8)
                wait(pe, head_kept, h)
                v0, v1 = mv_sb[:, 0, h, 0:257], mv_sb[:, 1, h, 0:257]
                pe.matmul(ps_t[:, 0, 0:257], scT[:, 0:128], v0, start=True, stop=True)
                pe.matmul(ps_t[:, 1, 0:257], scT[:, 128:256], v0, start=True, stop=False)
                pe.matmul(ps_t[:, 1, 0:257], scT[:, 256:384], v1, start=False, stop=True).then_inc(ml_out, 1)

            def even_side(s):
                for i, (slot, kind, b) in enumerate(E_TURNS):
                    if slot != s:
                        continue
                    t = T_E + i
                    cols = slice((b % 4) * P, (b % 4 + 1) * P)
                    if slot < LATE[0]:
                        ps_t_free(pe, 0, s)
                    if kind == "k":
                        pe.wait_ge(drained[0], 2)
                        turn(t, aknat[:, 0, b, :, :].rearrange("p a d -> p (a d)"),
                             aknat[:, 1, b, :, :].rearrange("p a d -> p (a d)"))
                    elif kind in ("q", "conv"):
                        n = 1 + b // 4 if kind == "q" else 3 + b // 4
                        pe.wait_ge(drained[n % 2], 2 * (n // 2) + 2)
                        turn(t, stage[:, n % 2, 0, cols], stage[:, n % 2, 1, cols])
                    elif b < 8:
                        pe.wait_ge(pair_made, b + 1)
                        turn(t, yp[:, 0, :], yp[:, 1, :])
                    else:
                        h, half = (b - 8) // 2, slice((b % 2) * P, (b % 2 + 1) * P)
                        pe.wait_ge(head_gated, h + 1)
                        turn(t, yB[:, 0, h, half], yB[:, 1, h, half])
                gates(s)
                if s - 1 in E_ATT + E_MLSTM:
                    ps_t_free(pe, 0, s)
                if s - 2 in E_ATT:
                    k = E_ATT.index(s - 2)
                    attend_pv(k, lambda t, hh: av[:, t, (k // 2) * 64:(k // 2) * 64 + 64])
                if s - 1 in E_ATT:
                    attend_turn(E_ATT.index(s - 1))
                if s in E_ATT:
                    even_scores(E_ATT.index(s))
                if s - 1 in E_MLSTM:
                    mlstm_values(E_MLSTM.index(s - 1))
                if s in E_MLSTM:
                    mlstm_scores(E_MLSTM.index(s))

            def odd_scores(k):
                wait(pe, probs_made, 4 * (8 + k))
                pe.wait_ge(pair_made, 8 + k)
                pe.wait_ge(bias_masked, k + 1)
                pe.wait_ge(odd_in, 32)
                operand_ready(turn_of(O_TURNS, T_O, "k", k))
                for hh in range(2):
                    half = slice(64 * hh, 64 * hh + 64)
                    s, b = ps_s[:, hh, :], biasT[:, k % 2, hh, :]
                    pe.matmul(s[:, 0:128], b[:, 0:P], flip[:], start=True, stop=False)
                    pe.matmul(s[:, 0:128], cqT[half, k, 0:P], ckT[half, k, 0:P], start=False, stop=True)
                    pe.matmul(s[:, 128:256], b[:, P:S], flip[:], start=True, stop=False)
                    pe.matmul(s[:, 256:384], b[:, 0:P], flip[:], start=False, stop=False)
                    ins = pe.matmul(s[:, 128:384], cqT[half, k, P:S], ckT[half, k, :], start=False, stop=True)
                ins.then_inc(scores_made, 1)

            def retention_scores(h):
                operand_ready(turn_of(O_TURNS, T_O, "rope", 4 + h if h < 4 else 8 + h))
                wait(pe, probs_made, 64)
                pe.wait_ge(pair_made, 16)
                wait(pe, ret_decayed, h - 1)
                pe.matmul(ps_s[:, h % 2, 0:256], rkT[:, h, 0:P], rqT[:, h, :], start=True, stop=True)
                pe.matmul(ps_s[:, h % 2, 256:384], rkT[:, h, P:S], rqT[:, h, P:S], start=True,
                          stop=True).then_inc(ret_scores, 1)

            def retention_values(h):
                pe.wait_ge(ret_decayed, h + 1)
                pe.wait_ge(drained[(C_O + 10 + h // 4) % 2], 2 * ((C_O + 10 + h // 4) // 2) + 2)
                wait(pe, probT_act, 16)
                wait(pe, probT_dve, 16)
                wait(pe, head_kept, 4 + h - 1)
                sc, o = scD[:, h % 2, :], ps_t[:, h % 2, :]
                v = slice(h * P, (h + 1) * P)
                pe.matmul(o[:, 0:128], sc[:, 0:128], rv[:, 0, v], start=True, stop=True)
                pe.matmul(o[:, 128:256], sc[:, 128:256], rv[:, 0, v], start=True, stop=False)
                pe.matmul(o[:, 128:256], sc[:, 256:384], rv[:, 1, v], start=False, stop=True).then_inc(ret_out, 1)

            def odd_side(s):
                for i, (slot, kind, b) in enumerate(O_TURNS):
                    if slot != s:
                        continue
                    t = T_O + i
                    cols = slice((b % 4) * P, (b % 4 + 1) * P)
                    if slot < LATE[1]:
                        ps_t_free(pe, 1, s)
                    if kind in ("q", "k"):
                        n = 2 * (b // 4) + (kind == "k")
                        pe.wait_ge(drained[(C_O + n) % 2], 2 * ((C_O + n) // 2) + 2)
                        turn(t, stage[:, n % 2, 0, cols], stage[:, n % 2, 1, cols])
                    elif kind == "rope":
                        n = 6 + b // 4
                        pe.wait_ge(rope_made, b // 4 + 1)
                        turn(t, stage[:, n % 2, 0, cols], stage[:, n % 2, 1, cols])
                    elif b < 8:
                        pe.wait_ge(pair_made, 8 + b + 1)
                        turn(t, yp[:, 0, :], yp[:, 1, :])
                    else:
                        pe.wait_ge(head_gated, 4 + b - 8 + 1)
                        turn(t, yD[:, 0, b - 8, :], yD[:, 1, b - 8, :])
                if s - 1 in O_ATT + O_RET:
                    ps_t_free(pe, 1, s)
                if s - 2 in O_ATT:
                    k = O_ATT.index(s - 2)
                    n = C_O + 4 + k // 4
                    pe.wait_ge(drained[n % 2], drains_after(n))
                    attend_pv(8 + k, lambda t, hh: cv[:, t, (2 * k + hh) * 64:(2 * k + hh) * 64 + 64])
                if s - 1 in O_ATT:
                    attend_turn(8 + O_ATT.index(s - 1))
                if s in O_ATT:
                    odd_scores(O_ATT.index(s))
                if s - 1 in O_RET:
                    retention_values(O_RET.index(s - 1))
                if s in O_RET:
                    retention_scores(O_RET.index(s))

            pe.wait_ge(first_in, 32)
            for b in range(8):
                if b % 4 == 0:
                    pe.wait_ge(x_in[b // 4], 16)
                x_turn(T_X + b, b)
            for s in range(36):
                if s % 4 == 0:
                    chunk_free(C_E + s // 4)
                if s < 4:
                    operand_ready(T_X + 4 * s + 3)
                unit(U_E + s, 4 * (s % 4), (C_E + s // 4) % 2, a_hi, a_lo, s % 4 == 0, s % 4 == 3)
                if s < 2:
                    pe.wait_ge(x_in[s + 2], 16)
                    for b in range(8 + 4 * s, 12 + 4 * s):
                        x_turn(T_X + b, b)
                even_side(s)

            def out_proj(u0, c0, turns, ty0, side, late, t0, cx):
                for n in range(NCH):
                    chunk_free(c0 + n)
                    for i in range(4):
                        if n == 0:
                            operand_ready(turn_of(turns, ty0, "y", 4 * i + 3))
                        unit(u0 + 4 * n + i, 4 * i, (c0 + n) % 2, y_hi, y_lo, i == 0, i == 3)
                        side(late + 4 * n + i)
                        if n >= 1:
                            x_ready(pe, cx, n)
                            x_turn(t0 + 4 * (n - 1) + i, 4 * (n - 1) + i)

            def last_x(s, t0, cx):
                if s < 2:
                    for b in (2 * s, 2 * s + 1):
                        x_ready(pe, cx, NCH)
                        x_turn(t0 + 12 + b, 12 + b)

            def swiglu(u0, c0, t0, tcx, cx, j):
                for i in range(8):
                    chunk = c0 + i // 4
                    if i % 4 == 0:
                        if isinstance(j, int):
                            chunk_free(chunk)
                        else:
                            pe.wait_ge(drained[chunk % 2], 2 * (chunk // 2) + j * 2)
                    if isinstance(j, int) and i < 4:
                        operand_ready(tcx + 4 * i + 3)
                    unit(u0 + i, 4 * (i % 4), chunk % 2, a_hi, a_lo, i % 4 == 0, i % 4 == 3, j)
                    if isinstance(j, int):
                        last_x(i, tcx, cx)
                    elif i < 4:
                        pe.wait_ge(drained[(c0 + 1) % 2], 2 * ((c0 + 1) // 2) + j * 2)
                        pe.wait_ge(turn_act, t0 + i - 7 + j * 4)
                        pe.wait_ge(turn_dve, t0 + i - 7 + j * 4)
                        dst = ring[region[t0 + i]]
                        cols = slice(i * P, (i + 1) * P)
                        pe.transpose(dst[:, 0, :], prod[:, 0, cols], ident[:])
                        pe.transpose(dst[:, 1, :], prod[:, 1, cols], ident[:]).then_inc(turned, 1)

            def down(u0, c0, t0, tcx, cx, n):
                chunk_free(c0 + n)
                for i in range(12):
                    if n == 0:
                        operand_ready(t0 + STARTS_DOWN[i] + UNITS_DOWN[i] - 1)
                    unit(u0 + 12 * n + i, STARTS_DOWN[i], (c0 + n) % 2, h_hi, h_lo,
                         i == 0, i == 11)
                    if n == 0 and i < 4:
                        pe.wait_ge(drained[(c0 - 1) % 2], drains_before(c0 + 1))
                        cols = slice(i * P, (i + 1) * P)
                        turn(t0 + FKT - 4 + i, prod[:, 0, cols], prod[:, 1, cols])
                    if n >= 1 and i < 4 and tcx is not None:
                        x_ready(pe, cx, n)
                        x_turn(tcx + 4 * (n - 1) + i, 4 * (n - 1) + i)

            out_proj(U_EO, C_EO, E_TURNS, T_E, even_side, 36, T_EO, C_EO)
            swiglu(U_F0, C_F0, T_F0, T_EO, C_EO, 0)
            with pe.Fori(1, FCH) as j:
                swiglu(U_F0, C_F0, T_F0, T_EO, C_EO, j)
            for n in range(NCH):
                down(U_D0, C_D0, T_F0, T_D0, C_D0, n)
            for s in range(56):
                if s % 4 == 0:
                    chunk_free(C_O + s // 4)
                if s < 4:
                    operand_ready(T_D0 + 4 * s + 3)
                unit(U_O + s, 4 * (s % 4), (C_O + s // 4) % 2, a_hi, a_lo, s % 4 == 0, s % 4 == 3)
                last_x(s, T_D0, C_D0)
                odd_side(s)
            out_proj(U_OO, C_OO, O_TURNS, T_O, odd_side, 56, T_OO, C_OO)
            swiglu(U_F1, C_F1, T_F1, T_OO, C_OO, 0)
            with pe.Fori(1, FCH) as j:
                swiglu(U_F1, C_F1, T_F1, T_OO, C_OO, j)
            for n in range(NCH):
                down(U_D1, C_D1, T_F1, None, C_D1, n)


def constants():
    i = np.arange(P)
    q, k = np.meshgrid(i, np.arange(S), indexing="ij")
    chunk_q, chunk_k = (q + P) // 64, k // 64
    ident = np.eye(P)
    upper = np.triu(np.ones((P, P)))
    win0 = np.where(i[:, None] // 64 >= i[None, :] // 64, 0.0, NEG)
    win1 = np.where((chunk_k <= chunk_q) & (chunk_k >= chunk_q - 1), 0.0, NEG)
    tri = np.where(i[None, :] >= i[:, None], 0.0, NEG)
    inv = np.float32(10000.0) ** (-np.arange(0, 128, 2, dtype=np.float32) / np.float32(128))
    ang = (np.arange(S, dtype=np.float32)[:, None] * inv[None, :]).astype(np.float64)
    trig = [f(ang).reshape(TT, P, 64).transpose(1, 0, 2).reshape(P, TT * 64) for f in (np.cos, np.sin)]
    const = np.concatenate([ident, upper, win0, win1, tri] + trig + [ident[::-1]], axis=1).astype(np.float32)
    gamma = 1.0 - 2.0 ** (-5.0 - np.arange(8))
    rel = np.arange(S)[None, None, :] - i[:, None, None]
    decay = np.where(rel >= 0, gamma[None, :, None] ** np.maximum(rel, 0), 0.0) * 128.0 ** -0.5
    sel = np.zeros((4, 4, P))
    for h in range(4):
        sel[h, h, :] = 1.0
    return const, decay.reshape(P, 8 * S).astype(np.float32), sel.astype(np.float32)


def kernel(x, ln_mix_g, ln_ffn_g, even_w_in, even_w_out, a_sinks, b_conv_w, b_conv_b, b_igate_bias,
           b_fgate_bias, b_norm_g, odd_w_in, odd_w_out, c_rel_bias, d_norm_g, ffn_w_gate, ffn_w_up,
           ffn_w_down, final_g):
    import numpy as _np
    import concourse.bacc as _bacc
    from concourse import mybir as _mybir
    from concourse.bass_utils import run_bass_kernel_spmd as _run

    def arr(a):
        return _np.ascontiguousarray(a)

    const, decay, sel = constants()
    gains = _np.stack([ln_mix_g[0], ln_ffn_g[0], ln_mix_g[1], ln_ffn_g[1]])
    conv = _np.concatenate([_np.asarray(b_conv_w[0]), _np.asarray(b_conv_b)], axis=0)
    rel = _np.asarray(c_rel_bias[0])
    rel = _np.concatenate([rel[:, 1:], _np.repeat(rel[:, 256:257], 127, axis=1)], axis=1)
    arrays = {
        "x": arr(_np.asarray(x).reshape(S, D)),
        "gains": arr(gains.reshape(4, KT, P).transpose(2, 0, 1)),
        "final_g": arr(final_g),
        "w_e": arr(_np.asarray(even_w_in)[0]),
        "w_eo": arr(_np.asarray(even_w_out)[0]),
        "w_o": arr(_np.asarray(odd_w_in)[0]),
        "w_oo": arr(_np.asarray(odd_w_out)[0]),
        "w_gate": arr(ffn_w_gate),
        "w_up": arr(ffn_w_up),
        "w_down": arr(ffn_w_down),
        "sinks": arr(_np.repeat(_np.asarray(a_sinks).reshape(8, 1, 2), 2, axis=1)),
        "conv": arr(conv.reshape(5, 8, P).transpose(2, 1, 0)),
        "gate_bias": arr(_np.concatenate([_np.asarray(b_igate_bias)[0], _np.asarray(b_fgate_bias)[0]])),
        "b_norm_g": arr(_np.asarray(b_norm_g)[0]),
        "d_norm_g": arr(_np.asarray(d_norm_g)[0]),
        "rel": arr(rel),
        "const": const,
        "dtab": decay,
        "sel": sel,
    }
    nc = _bacc.Bacc("TRN2", target_bir_lowering=False, num_devices=1, dynamic_dma_scratch_size=1024)
    aps = {n: nc.dram_tensor(n, a.shape, _mybir.dt.from_np(a.dtype), kind="ExternalInput").ap()
           for n, a in arrays.items()}
    out = nc.dram_tensor("out", (S, D), _mybir.dt.float32, kind="ExternalOutput").ap()
    build(nc, out=out, **aps)
    r = _run(nc, [arrays], core_ids=[0])
    return r.results[0]["out"].reshape(1, S, D)
```

```python
import concourse.bass as bass
from concourse import mybir
from contextlib import ExitStack

import numpy as np

F32 = mybir.dt.float32
F32R = mybir.dt.float32r
BF16 = mybir.dt.bfloat16
ALU = mybir.AluOpType
ACT = mybir.ActivationFunctionType
AX = mybir.AxisListType

P = 128
S = 256
TT = S // P
D = 2048
KT = D // P
CW = 512
EPS = 1e-6
NEG = -1e30
FF = 5632
FKT = FF // P
FCH = FF // CW
EVEN_IN, ODD_IN = 4616, 7168
NCH = D // CW

E_ORDER = [2, 0, 1, 3, 4, 5, 6, 7, 8]
O_ORDER = [0, 2, 1, 3, 4, 5, 6, 8, 7, 9, 10, 11, 12, 13]
UNITS_IN = [4] * 4
UNITS_DOWN = [4] * 8 + [3] * 4
STARTS_DOWN = [sum(UNITS_DOWN[:i]) for i in range(len(UNITS_DOWN))]

U_E = 0
U_EO = U_E + 4 * len(E_ORDER)
U_F0 = U_EO + 4 * NCH
U_D0 = U_F0 + 8 * FCH
U_O = U_D0 + 12 * NCH
U_OO = U_O + 4 * len(O_ORDER)
U_F1 = U_OO + 4 * NCH
U_D1 = U_F1 + 8 * FCH
UNITS = U_D1 + 12 * NCH
UNIT_ROWS = [4] * U_D0 + UNITS_DOWN * NCH + [4] * (U_D1 - U_O) + UNITS_DOWN * NCH
C_E = 0
C_EO = len(E_ORDER)
C_F0 = C_EO + NCH
C_D0 = C_F0 + 2 * FCH
C_O = C_D0 + NCH
C_OO = C_O + len(O_ORDER)
C_F1 = C_OO + NCH
C_D1 = C_F1 + 2 * FCH

E_TURNS = sorted(
    [(4 + i, "k", i) for i in range(4)] + [(8 + i, "q", i) for i in range(8)]
    + [(17 + 2 * i, "conv", i) for i in range(8)]
    + [(16 + 2 * i, "y", i) for i in range(8)]
    + [(s, "y", 8 + i) for i, s in enumerate((35, 36, 36, 36, 37, 37, 37, 37))])
RQK_SLOTS = [28, 30, 31, 33, 34, 36, 37, 39, 40, 42, 43, 45, 46, 47, 48, 49]
O_TURNS = sorted(
    [(4 + i, "q", i) for i in range(4)] + [(8 + i, "k", i) for i in range(4)]
    + [(12 + i, "q", 4 + i) for i in range(4)] + [(16 + i, "k", 4 + i) for i in range(4)]
    + [(s, "rope", i) for i, s in enumerate(RQK_SLOTS)]
    + [(23 + 3 * i, "y", i) for i in range(8)]
    + [(s, "y", 8 + i) for i, s in enumerate((53, 54, 55, 56, 57, 57, 57, 57))])
T_X = 0
T_E = T_X + KT
T_EO = T_E + len(E_TURNS)
T_F0 = T_EO + KT
T_D0 = T_F0 + FKT
T_O = T_D0 + KT
T_OO = T_O + len(O_TURNS)
T_F1 = T_OO + KT

E_ATT = [13 + 2 * k for k in range(8)]
O_ATT = [20 + 3 * k for k in range(8)]
E_MLSTM = [29, 30, 31, 33]
O_RET = [44, 45, 46, 47, 50, 51, 52, 53]
LATE = 36, 56

LOG_TERMS = 8
WARM_UP = 9, 5, 0
MLSTM_SCALE = 128.0 ** -0.5 * 0.25


def turn_of(turns, base, kind, i):
    return base + [t[1:] for t in turns].index((kind, i))


def drains_before(chunk):
    return 2 * (chunk // 2)


def drains_after(chunk):
    return 2 * (chunk // 2) + 2


def half_rows(h):
    return min(2, UNIT_ROWS[h // 2] - 2 * (h % 2))


def split_ahead(split, u, j=0):
    for h in (2 * u + 3, 2 * u + 4):
        if h < 2 * UNITS:
            split(h, j)


def wait(eng, sem, value):
    if isinstance(value, int) and value <= 0:
        return
    eng.wait_ge(sem, value)


def build(nc, x, gains, final_g, w_e, w_eo, w_o, w_oo, w_gate, w_up, w_down, sinks, conv,
          gate_bias, b_norm_g, d_norm_g, rel, const, dtab, sel, out):
    ctx = ExitStack()
    with ctx:
        def sb(name, shape, dt=F32):
            return ctx.enter_context(nc.sbuf_tensor(name, shape, dt))

        def sem(name):
            return ctx.enter_context(nc.semaphore(name))

        xs = sb("xs", [P, TT, D])
        a_hi = sb("a_hi", [P, KT, S], F32R)
        a_lo = sb("a_lo", [P, KT, S], F32R)
        raw = sb("raw", [P, 4, 4, CW])
        w_hi = sb("w_hi", [P, 4, 2, CW], F32R)
        w_lo = sb("w_lo", [P, 4, 2, CW], F32R)
        ident = sb("ident", [P, P])
        ident_b = sb("ident_b", [P, P], BF16)
        gain = sb("gain", [P, 4, KT])
        ssq = sb("ssq", [P, 5, TT, NCH])
        ssum = sb("ssum", [P, 5, TT])
        half_ms = sb("half_ms", [P, 5, TT])
        root = sb("root", [P, 5, TT])
        rstd = sb("rstd", [P, 5, 3, TT])
        eps = sb("eps", [P, 1])
        table_ready = sb("table_ready", [P, 1])
        ones = sb("ones", [P, P])
        junk = sb("junk", [P, CW], BF16)
        nm = sb("nm", [P, 2, 2])
        mx = sb("mx", [P, 2, 2])
        psum_p = sb("psum_p", [P, 2, 2])
        sinkv = sb("sinkv", [P, 8, 2, 2])
        nsink = sb("nsink", [P, 8, 2, 2])
        sshift = sb("sshift", [P, 2, 2])
        es = sb("es", [P, 2, 2])
        den = sb("den", [P, 2, 2])
        rden = sb("rden", [P, 2, 2])
        stats = sb("stats", [P, 8, TT, 6])
        mv = sb("mv", [P, 8, TT, 2])
        sd = sb("sd", [P, 8, TT])
        rs = sb("rs", [P, 8, TT])
        hnorm = sb("hnorm", [P, 3, 4, TT])
        convp = sb("convp", [P, 8, 5])
        gbias = sb("gbias", [P, 8])

        base = -(-nc.sbuf_base // 64) * 64

        class Region:

            def __init__(self, at):
                self.at = at

            def put(self, name, shape, dt=F32, at=None):
                size = int(np.prod(shape[1:])) * (2 if dt == BF16 else 4)
                start = self.at if at is None else at
                if at is None:
                    self.at += -(-size // 32) * 32
                return nc.alloc_sbuf_tensor_at(name, shape, dt, offset=start), start

        ffn = Region(base)
        h_hi, _ = ffn.put("h_hi", [P, FKT, S], F32R)
        h_lo, _ = ffn.put("h_lo", [P, FKT, S], F32R)
        silu, silu_at = ffn.put("silu", [P, TT, CW])
        prod, _ = ffn.put("prod", [P, TT, CW])
        final_gain, _ = ffn.put("final_gain", [P, D], at=silu_at)

        mix = Region(base)
        y_hi, _ = mix.put("y_hi", [P, KT, S], F32R)
        y_lo, _ = mix.put("y_lo", [P, KT, S], F32R)
        stage, _ = mix.put("stage", [P, 2, TT, CW])
        yp, _ = mix.put("yp", [P, TT, P])
        prob, prob_at = mix.put("prob", [P, 2, 384])
        probT, probT_at = mix.put("probT", [P, 2, 384])
        gfac, gfac_at = mix.put("gfac", [P, TT, 1024])
        split_at = mix.at

        ev = Region(split_at)
        aqT, aqT_at = ev.put("aqT", [P, 8, S])
        akT, _ = ev.put("akT", [P, 4, S])
        aknat, _ = ev.put("aknat", [P, TT, 4, 2, 64])
        av, _ = ev.put("av", [P, TT, 4 * 64])
        cbuf, _ = ev.put("cbuf", [P, 3 + S + 1])
        cacc, _ = ev.put("cacc", [P, 2, S])
        cth, _ = ev.put("cth", [P, S])
        mqk, _ = ev.put("mqk", [P, 8, S])
        mv_sb, _ = ev.put("mv_sb", [P, TT, 4, 260])
        gnorm, _ = ev.put("gnorm", [P, 1024])
        gw, _ = ev.put("gw", [P, KT, 8])
        gw_hi, _ = ev.put("gw_hi", [P, KT, 8], F32R)
        gw_lo, _ = ev.put("gw_lo", [P, KT, 8], F32R)
        upper, _ = ev.put("upper", [P, P])
        win, _ = ev.put("win", [P, 384])
        tri_b, _ = ev.put("tri_b", [P, P], BF16)
        selr, _ = ev.put("selr", [4, 4, P])
        negm, _ = ev.put("negm", [4, S])
        gx, _ = ev.put("gx", [P, TT, 8])
        gsc, _ = ev.put("gsc", [P, 8, TT, 4])
        yB, _ = ev.put("yB", [P, TT, 4, 256], at=aqT_at)
        cmax, _ = ev.put("cmax", [4, 2, P + S], at=prob_at)
        wgt, _ = ev.put("wgt", [P, 384], at=prob_at)
        scT, _ = ev.put("scT", [P, 384], at=prob_at + 1536)
        tri_f, _ = ev.put("tri_f", [P, P], at=probT_at)
        gateT, _ = ev.put("gateT", [8, S], at=probT_at + 2048)
        ev_end = ev.at

        od = Region(split_at - 8192)
        cqT, cqT_at = od.put("cqT", [P, 8, S], at=split_at)
        od.at = split_at + 8192
        ckT, ckT_at = od.put("ckT", [P, 8, S])
        cv, cv_at = od.put("cv", [P, TT, 1024])
        rqT, _ = od.put("rqT", [P, 8, S])
        rkT, _ = od.put("rkT", [P, 8, S])
        rv, _ = od.put("rv", [P, TT, 1024])
        rtmp, _ = od.put("rtmp", [P, 2, TT, 4, 64], at=gfac_at)
        biasT, _ = od.put("biasT", [P, 2, 2, S], at=gfac_at + 4096)
        trig, _ = od.put("trig", [P, 2, TT, 64])
        flip, _ = od.put("flip", [P, P])
        yD, _ = od.put("yD", [P, TT, 8, 128], at=cqT_at)
        decay, _ = od.put("decay", [P, 8, S], at=ckT_at)
        scD, _ = od.put("scD", [P, 2, 384], at=prob_at)
        gnorm_o, _ = od.put("gnorm_o", [P, 1024], at=cv_at)
        end = max(ffn.at, ev_end, od.at)
        assert end <= nc.sbuf_usable_end, (end, nc.sbuf_usable_end)
        ctx.enter_context(nc.sbuf_tensor("fence", [P, (end - nc.sbuf_base) // 4], F32))

        ps_g = ctx.enter_context(nc.psum_tensor("ps_g", [P, 2, TT, CW], F32))
        ps_s = ctx.enter_context(nc.psum_tensor("ps_s", [P, 2, CW], F32))
        ps_t = ctx.enter_context(nc.psum_tensor("ps_t", [P, 2, CW], F32))
        ring = [ps_s[:, 0, 0:S], ps_s[:, 1, 0:S], ps_t[:, 0, 0:S], ps_t[:, 1, 0:S]]
        ring = [r.rearrange("p (t c) -> p t c", t=TT) for r in ring]
        beside = ps_t[:, :, 384:512]
        region = {}
        n = 0
        for t0, turns in ((T_X, KT), (T_E, E_TURNS), (T_EO, KT), (T_F0, FKT), (T_D0, KT),
                          (T_O, O_TURNS), (T_OO, KT), (T_F1, FKT)):
            if isinstance(turns, int):
                for t in range(turns):
                    region[t0 + t] = (n + t) % 4
                n += turns
            else:
                late = LATE[t0 == T_O]
                for t, (slot, _, _) in enumerate(turns):
                    region[t0 + t] = "beside" if slot < late else n % 4
                    n += slot >= late

        def turn_psum(t):
            return beside if region[t] == "beside" else ring[region[t]]

        def banks(t):
            return {2, 3} if region[t] == "beside" else {region[t]}

        def turn_before(t):
            return max((u for u in range(t) if banks(u) & banks(t)), default=-1)

        params_in = sem("params_in")
        first_in = sem("first_in")
        x_in = [sem(f"x_in{n}") for n in range(NCH)]
        first_half_in = sem("first_half_in")
        raw_in = [sem(f"raw_in{i}") for i in range(4)]
        hi_made = sem("hi_made")
        lo_made = sem("lo_made")
        half_used = sem("half_used")
        drained = [sem("drained0"), sem("drained1")]
        turned = sem("turned")
        turn_act = sem("turn_act")
        turn_dve = sem("turn_dve")
        squares = sem("squares")
        sum_made = sem("sum_made")
        root_made = sem("root_made")
        rstd_made = sem("rstd_made")
        consts_made = sem("consts_made")
        zeros_made = sem("zeros_made")
        ones_made = sem("ones_made")
        scores_made = sem("scores_made")
        max_made = sem("max_made")
        probs_made = sem("probs_made")
        sinks_made = sem("sinks_made")
        probs_turned = sem("probs_turned")
        probT_act = sem("probT_act")
        probT_dve = sem("probT_dve")
        pv_made = sem("pv_made")
        pair_made = sem("pair_made")
        bias_in = [sem("bias_in0"), sem("bias_in1")]
        bias_masked = sem("bias_masked")
        gatew_hi = sem("gatew_hi")
        gatew_lo = sem("gatew_lo")
        gates_mm = sem("gates_mm")
        gates_dve = sem("gates_dve")
        gates_act = sem("gates_act")
        conv_made = sem("conv_made")
        tanh_made = sem("tanh_made")
        qk_made = sem("qk_made")
        ml_scores = sem("ml_scores")
        ml_weights = sem("ml_weights")
        ml_weighted = sem("ml_weighted")
        ml_out = sem("ml_out")
        head_kept = sem("head_kept")
        rope_pool = sem("rope_pool")
        rope_dve = sem("rope_dve")
        decay_in = sem("decay_in")
        ret_scores = sem("ret_scores")
        ret_decayed = sem("ret_decayed")
        ret_out = sem("ret_out")
        head_root = sem("head_root")
        head_normed = sem("head_normed")
        gate_made = sem("gate_made")
        head_gated = sem("head_gated")
        odd_in = sem("odd_in")
        dve_step = sem("dve_step")
        pool_step = sem("pool_step")
        final_g_in = sem("final_g_in")
        x_gained = sem("x_gained")
        out_dve = sem("out_dve")
        out_act = sem("out_act")
        out_stored = sem("out_stored")

        PARAMS = 9 * 16

        def odd_stage_free(n):
            former = {2: ("q", 3), 3: ("k", 3), 6: ("q", 7), 7: ("k", 7), 8: ("rope", 3), 9: ("rope", 7)}[n]
            return turn_of(O_TURNS, T_O, *former) + 1

        def ps_t_free(pe, odd, s):
            turns, base = (O_TURNS, T_O) if odd else (E_TURNS, T_E)
            n = base + sum(slot < s for slot, _, _ in turns)
            pe.wait_ge(turn_act, n)
            pe.wait_ge(turn_dve, n)
            pairs = 8 * odd + sum(a + 1 < s for a in (O_ATT if odd else E_ATT))
            wait(pe, probT_act, pairs)
            wait(pe, probT_dve, pairs)
            wait(pe, head_kept, 4 * odd + sum(a + 1 < s for a in (O_RET if odd else E_MLSTM)))

        def ps_t_settled(eng, odd, s):
            if s - 1 in (O_ATT if odd else E_ATT):
                eng.wait_ge(probs_turned, 8 * odd + (O_ATT if odd else E_ATT).index(s - 1) + 1)
            if not odd and s - 1 in E_MLSTM:
                eng.wait_ge(ml_out, E_MLSTM.index(s - 1) + 1)
            if odd and s - 1 in O_RET:
                eng.wait_ge(ret_out, O_RET.index(s - 1) + 1)

        def x_ready(eng, c0, n):
            eng.wait_ge(drained[(c0 + n - 1) % 2], drains_after(c0 + n - 1))

        block = ctx.enter_context(nc.Block())

        @block.sync
        def _(sp):
            def load(u, slot, rows, src):
                wait(sp, hi_made, 2 * (u - 3))
                wait(sp, lo_made, 2 * (u - 3))
                sp.dma_start(raw[:, slot, 0:rows, :], src).then_inc(raw_in[slot], 16)

            def unit_src(w, k0, rows, c0):
                return w[k0 * P:(k0 + rows) * P, c0].rearrange("(k p) c -> p k c", p=P)

            def in_units(u0, w, chunks):
                for n, c in enumerate(chunks):
                    for i in range(4):
                        load(u0 + 4 * n + i, i, 4, unit_src(w, 4 * i, 4, slice(c * CW, (c + 1) * CW)))

            def ffn_units(layer, u0, u1):
                with sp.Fori(0, FCH) as j:
                    for i in range(8):
                        w = (w_gate, w_up)[i // 4][layer]
                        load(u0 + i + j * 8, i % 4, 4, unit_src(w, 4 * (i % 4), 4, bass.ds(j * CW, CW)))
                with sp.Fori(0, NCH) as n:
                    for i, rows in enumerate(UNITS_DOWN):
                        load(u1 + i + n * 12, i % 4, rows,
                             unit_src(w_down[layer], STARTS_DOWN[i], rows, bass.ds(n * CW, CW)))

            sp.dma_start(ident[:], const[:, 0:P]).then_inc(first_in, 16)
            sp.dma_start(gain[:], gains).then_inc(first_in, 16)
            for i in range(4):
                cols = slice(i * CW, (i + 1) * CW)
                sp.dma_start(xs[:, :, cols], x[:, cols].rearrange("(t p) c -> p t c", p=P)).then_inc(x_in[i], 16)
                wcols = slice(E_ORDER[0] * CW, (E_ORDER[0] + 1) * CW)
                if i == 0:
                    sp.dma_start(raw[:, 0, 0:2, :], unit_src(w_e, 0, 2, wcols)).then_inc(first_half_in, 16)
                    sp.dma_start(raw[:, 0, 2:4, :], unit_src(w_e, 2, 2, wcols)).then_inc(raw_in[0], 16)
                else:
                    load(U_E + i, i, 4, unit_src(w_e, 4 * i, 4, wcols))
            for dst, src in ((gw, w_e[:, 9 * CW:EVEN_IN].rearrange("(k p) c -> p k c", p=P)),
                             (upper, const[:, P:2 * P]), (win, const[:, 2 * P:5 * P]),
                             (tri_f, const[:, 5 * P:6 * P]), (sinkv, sinks.partition_broadcast(P)),
                             (convp, conv), (gbias, gate_bias.partition_broadcast(P)), (selr, sel),
                             (gnorm, b_norm_g.partition_broadcast(P))):
                sp.dma_start(dst[:], src).then_inc(params_in, 16)
            in_units(U_E + 4, w_e, E_ORDER[1:])
            in_units(U_EO, w_eo, range(NCH))
            ffn_units(0, U_F0, U_D0)
            in_units(U_O, w_o, O_ORDER)
            in_units(U_OO, w_oo, range(NCH))
            ffn_units(1, U_F1, U_D1)
            for h in range(2):
                cols = slice(h * 1024, (h + 1) * 1024)
                for t, made in enumerate((out_dve, out_act)):
                    sp.wait_ge(made, h + 1)
                    sp.dma_start(out[t * P:(t + 1) * P, cols], xs[:, t, cols]).then_inc(out_stored, 16)
            sp.wait_ge(out_stored, 4 * 16)

        @block.scalar
        def _(act):
            def split_hi(h, j=0):
                rows, slot, r0 = half_rows(h), h // 2 % 4, 2 * (h % 2)
                if h == 0:
                    act.wait_ge(first_half_in, 16)
                else:
                    act.wait_ge(raw_in[slot], 16 * (h // 8 + 1) + j * 32)
                wait(act, half_used, h - 3 + j * 16)
                act.activation(w_hi[:, h % 4, 0:rows, :], raw[:, slot, r0:r0 + rows, :],
                               ACT.Copy).then_inc(hi_made, 1)

            def turn_hi(t, src, dst, scale=None):
                act.wait_ge(turned, t + 1)
                if scale is None:
                    act.activation(dst, src, ACT.Copy).then_inc(turn_act, 1)
                else:
                    act.activation(dst, src, ACT.Identity, scale=scale).then_inc(turn_act, 1)

            def x_turn_hi(t, norm, kt):
                src = turn_psum(t)
                turn_hi(t, src, a_hi[:, kt, :].rearrange("p (t c) -> p t c", t=TT),
                        gain[:, norm, kt:kt + 1])

            def squares_of(norm, n, c0=None):
                for t in range(TT):
                    if c0 is not None:
                        act.wait_ge(drained[(c0 + n) % 2], drains_after(c0 + n) - 1 + t)
                    wait(act, squares, 8 * norm + 2 * n + t)
                    act.activation(junk[:], xs[:, t, n * CW:(n + 1) * CW], ACT.Square,
                                   accum_out=ssq[:, norm, t, n:n + 1]).then_inc(squares, 1)

            def root_of(norm):
                act.wait_ge(sum_made, norm + 1)
                act.activation(root[:, norm, :], ssum[:, norm, :], ACT.Sqrt, bias=eps[:, 0:1],
                               scale=1.0 / D).then_inc(root_made, 1)

            def attend_scores(k, gk):
                act.wait_ge(scores_made, gk + 1)
                act.wait_ge(max_made, gk + 1)
                wait(act, probs_turned, gk)
                for tt, (a, b) in enumerate(((0, 128), (128, 384))):
                    for hh in range(2):
                        scores = prob if gk < 8 else ps_s
                        act.activation(prob[:, hh, a:b], scores[:, hh, a:b], ACT.Exp,
                                       bias=nm[:, tt, hh:hh + 1],
                                       accum_out=psum_p[:, tt, hh:hh + 1]).then_inc(probs_made, 1)
                if gk < 8:
                    act.activation(es[:], sshift[:], ACT.Exp).then_inc(sinks_made, 1)

            def attend_turned(gk):
                act.wait_ge(probs_turned, gk + 1)
                wait(act, pv_made, gk)
                act.activation(probT[:, 0, :], ps_t[:, 0, 0:384], ACT.Copy).then_inc(probT_act, 1)

            def head_roots(n, heads):
                act.wait_ge(head_kept, n)
                act.activation(sd[:, heads, :], mv[:, heads, :, 1], ACT.Sqrt,
                               bias=eps[:, 0:1]).then_inc(head_root, 1)

            def even_drain(n):
                c = E_ORDER[n]
                pair = (C_E + n) % 2
                act.wait_ge(half_used, 2 * (U_E + 4 * n + 4))
                act.wait_ge(rstd_made, 1)
                ps = ps_g[:, pair, 0, :]
                r1, r8 = rstd[:, 0, 0, 0:1], rstd[:, 0, 1, 0:1]
                if c == 2:
                    for d in range(2):
                        act.activation(aknat[:, 0, :, d, :], ps[:, 0:256].rearrange("p (h d) -> p h d", d=64),
                                       ACT.Identity, scale=r1)
                    act.activation(av[:, 0, :], ps[:, 256:512], ACT.Identity,
                                   scale=r1).then_inc(drained[pair], 1)
                elif c in (0, 1):
                    act.activation(stage[:, n % 2, 0, :], ps, ACT.Identity, scale=r8).then_inc(drained[pair], 1)
                elif c in (3, 4):
                    act.wait_ge(turned, T_E + 4 + 4 * (n - 2))
                    act.activation(stage[:, n % 2, 0, :], ps, ACT.Identity, scale=r1).then_inc(drained[pair], 1)
                elif c in (5, 6):
                    h = 2 * (c - 5)
                    act.activation(mv_sb[:, 0, h:h + 2, 0:256], ps.rearrange("p (h d) -> p h d", h=2),
                                   ACT.Identity, scale=r1).then_inc(drained[pair], 1)
                else:
                    for t in range(TT):
                        act.activation(gfac[:, t, (c - 7) * CW:(c - 6) * CW], ps_g[:, pair, t, :], ACT.Tanh,
                                       scale=rstd[:, 0, 2, t:t + 1]).then_inc(drained[pair], 1)

            def even_side(s):
                for i, (slot, kind, b) in enumerate(E_TURNS):
                    if slot != s:
                        continue
                    t = T_E + i
                    src = turn_psum(t)
                    ps_t_settled(act, 0, s)
                    if kind == "y":
                        turn_hi(t, src, y_hi[:, b, :].rearrange("p (t c) -> p t c", t=TT))
                    elif kind == "conv":
                        wait(act, conv_made, b)
                        act.wait_ge(zeros_made, 3)
                        turn_hi(t, src[:, 0, :], cbuf[:, 3:3 + P])
                    else:
                        turn_hi(t, src[:, 0, :], (akT if kind == "k" else aqT)[:, b, 0:P])
                if s == 5:
                    act.wait_ge(gates_dve, 2)
                    act.activation(gsc[:, 1, :, :], gsc[:, 0, :, :], ACT.Exp).then_inc(gates_act, 1)
                if s == 10:
                    act.wait_ge(gates_dve, 6)
                    act.activation(gsc[:, 7, :, :], gsc[:, 6, :, :], ACT.Exp, scale=-1.0).then_inc(gates_act, 1)
                if s in E_ATT:
                    attend_scores(E_ATT.index(s), E_ATT.index(s))
                if s - 1 in E_ATT:
                    attend_turned(E_ATT.index(s - 1))
                for b in range(8):
                    if s == 18 + 2 * b:
                        act.wait_ge(conv_made, b + 1)
                        wait(act, qk_made, b)
                        act.activation(cth[:], cacc[:, b % 2, :], ACT.Tanh, scale=0.5).then_inc(tanh_made, 1)
                if s in E_MLSTM:
                    h = E_MLSTM.index(s)
                    act.wait_ge(ml_scores, h + 1)
                    act.wait_ge(pair_made, 8)
                    wait(act, ml_weighted, h)
                    act.activation(wgt[:, 0:256], ps_s[:, 1, 0:256], ACT.Exp,
                                   bias=gsc[:, 4, 0, h:h + 1]).then_inc(ml_weights, 1)
                    act.activation(wgt[:, 256:384], ps_s[:, 1, 256:384], ACT.Exp,
                                   bias=gsc[:, 4, 1, h:h + 1]).then_inc(ml_weights, 1)
                if s < 36 and s % 4 == 3:
                    even_drain(s // 4)
                if s in (33, 35):
                    head_roots(s - 31, slice(s - 33, s - 31))

            def odd_drain(n):
                c = O_ORDER[n]
                pair = (C_O + n) % 2
                act.wait_ge(half_used, 2 * (U_O + 4 * n + 4))
                act.wait_ge(rstd_made, 3)
                ps = ps_g[:, pair, 0, :]
                r1, r8 = rstd[:, 2, 0, 0:1], rstd[:, 2, 1, 0:1]
                if c < 4 or 6 <= c < 10:
                    if n in (2, 3, 6, 7, 8, 9):
                        act.wait_ge(turned, odd_stage_free(n))
                    act.activation(stage[:, n % 2, 0, :], ps, ACT.Identity,
                                   scale=r8 if c < 2 else r1).then_inc(drained[pair], 1)
                elif c < 6:
                    act.activation(cv[:, 0, (c - 4) * CW:(c - 3) * CW], ps, ACT.Identity,
                                   scale=r1).then_inc(drained[pair], 1)
                elif c < 12:
                    act.activation(rv[:, 0, (c - 10) * CW:(c - 9) * CW], ps, ACT.Identity,
                                   scale=r1).then_inc(drained[pair], 1)
                else:
                    for t in range(TT):
                        act.activation(gfac[:, t, (c - 12) * CW:(c - 11) * CW], ps_g[:, pair, t, :], ACT.Silu,
                                       scale=rstd[:, 2, 0, t:t + 1]).then_inc(drained[pair], 1)

            def load_bias(k):
                if k >= 2:
                    act.wait_ge(scores_made, 8 + k - 1)
                for hh in range(2):
                    src = bass.AP(rel.tensor, (2 * k + hh) * 383, [[1, P], [1, S]])
                    act.dma_start(biasT[:, k % 2, hh, :], src).then_inc(bias_in[k % 2], 16)

            def odd_side(s):
                for i, (slot, kind, b) in enumerate(O_TURNS):
                    if slot != s:
                        continue
                    t = T_O + i
                    src = turn_psum(t)
                    ps_t_settled(act, 1, s)
                    if kind == "y":
                        turn_hi(t, src, y_hi[:, b, :].rearrange("p (t c) -> p t c", t=TT))
                    elif kind == "rope":
                        g, h = b // 4, b % 4
                        turn_hi(t, src[:, 0, :], (rqT, rkT)[g % 2][:, 4 * (g // 2) + h, 0:P])
                    else:
                        turn_hi(t, src[:, 0, :], (cqT if kind == "q" else ckT)[:, b, 0:P])
                if s == 4:
                    load_bias(0)
                    load_bias(1)
                    act.dma_start(trig[:].rearrange("p a t c -> p (a t c)"),
                                  const[:, 768:1024]).then_inc(odd_in, 16)
                    act.dma_start(flip[:], const[:, 1024:1152]).then_inc(odd_in, 16)
                if s in O_ATT:
                    k = O_ATT.index(s)
                    attend_scores(k, 8 + k)
                    if k < 6:
                        load_bias(k + 2)
                    if k == 7:
                        act.dma_start(decay[:].rearrange("p h c -> p (h c)"), dtab).then_inc(decay_in, 16)
                if s - 1 in O_ATT:
                    attend_turned(8 + O_ATT.index(s - 1))
                if s == 44:
                    act.wait_ge(pv_made, 16)
                    act.dma_start(gnorm_o[:], d_norm_g.partition_broadcast(P)).then_inc(odd_in, 16)
                if s < 56 and s % 4 == 3:
                    odd_drain(s // 4)
                if s == 49:
                    head_roots(8, slice(0, 4))
                if s == 55:
                    head_roots(12, slice(4, 8))

            act.wait_ge(zeros_made, 1)
            act.activation(table_ready[:], eps[:], ACT.Copy)
            act.wait_ge(first_in, 32)
            for b in range(8):
                x_turn_hi(T_X + b, 0, b)
                if b == 3:
                    split_hi(0)
                    split_hi(1)
            split_hi(2)
            for s in range(36):
                split_ahead(split_hi, U_E + s)
                if s < 2:
                    for b in range(8 + 4 * s, 12 + 4 * s):
                        x_turn_hi(T_X + b, 0, b)
                    for n in (2 * s, 2 * s + 1):
                        act.wait_ge(x_in[n], 16)
                        squares_of(0, n)
                if s == 2:
                    root_of(0)
                if s == 3:
                    act.wait_ge(params_in, PARAMS)
                    act.activation(gw_hi[:], gw[:], ACT.Copy).then_inc(gatew_hi, 1)
                    act.activation(ident_b[:], ident[:], ACT.Copy).then_inc(consts_made, 1)
                    act.activation(tri_b[:], tri_f[:], ACT.Copy).then_inc(consts_made, 1)
                even_side(s)

            def out_proj(u0, side, late, t0, norm, cx):
                for n in range(NCH):
                    for i in range(4):
                        split_ahead(split_hi, u0 + 4 * n + i)
                        side(late + 4 * n + i)
                        if n >= 1:
                            x_turn_hi(t0 + 4 * (n - 1) + i, norm, 4 * (n - 1) + i)
                        if n >= 1 and i == 3:
                            squares_of(norm, n - 1, cx)

            def last_x(s, t0, norm, cx):
                if s < 2:
                    for b in (2 * s, 2 * s + 1):
                        x_turn_hi(t0 + 12 + b, norm, 12 + b)
                if s == 2:
                    squares_of(norm, NCH - 1, cx)
                    root_of(norm)

            def swiglu(u0, c0, t0, norm, tcx, cx, j):
                for i in range(8):
                    split_ahead(split_hi, u0 + i, j)
                    if isinstance(j, int):
                        last_x(i, tcx, norm, cx)
                    elif i < 4:
                        t = t0 + i + j * 4 - 4
                        act.wait_ge(turned, t + 1)
                        act.activation(h_hi[:, bass.ds(j * 4 + (i - 4), 1), :].rearrange("p a (t c) -> p (a t) c", t=TT),
                                       ring[region[t0 + i]], ACT.Copy).then_inc(turn_act, 1)
                    if i == 3:
                        act.wait_ge(half_used, 2 * (u0 + 4 + j * 8))
                        act.wait_ge(drained[(c0 + 1) % 2], 2 * ((c0 + 1) // 2) + j * 2)
                        act.wait_ge(rstd_made, norm + 1)
                        for t in range(TT):
                            act.activation(silu[:, t, :], ps_g[:, c0 % 2, t, :], ACT.Silu,
                                           scale=rstd[:, norm, 0, t:t + 1]).then_inc(drained[c0 % 2], 1)

            def down(u0, t0, tcx, norm, cx, n):
                for i in range(12):
                    split_ahead(split_hi, u0 + 12 * n + i)
                    if n == 0 and i < 4:
                        t = t0 + FKT - 4 + i
                        turn_hi(t, turn_psum(t), h_hi[:, FKT - 4 + i, :].rearrange("p (t c) -> p t c", t=TT))
                    if n >= 1 and i < 4 and tcx is not None:
                        x_turn_hi(tcx + 4 * (n - 1) + i, norm, 4 * (n - 1) + i)
                    if n >= 1 and i == 4:
                        squares_of(norm, n - 1, cx)
                    if n == 0 and i == 4 and tcx is None:
                        act.wait_ge(turned, t0 + FKT)
                        act.dma_start(final_gain[:], final_g.partition_broadcast(P)).then_inc(final_g_in, 16)

            out_proj(U_EO, even_side, 36, T_EO, 1, C_EO)
            swiglu(U_F0, C_F0, T_F0, 1, T_EO, C_EO, 0)
            with act.Fori(1, FCH) as j:
                swiglu(U_F0, C_F0, T_F0, 1, T_EO, C_EO, j)
            for n in range(NCH):
                down(U_D0, T_F0, T_D0, 2, C_D0, n)
            for s in range(56):
                split_ahead(split_hi, U_O + s)
                last_x(s, T_D0, 2, C_D0)
                odd_side(s)
            out_proj(U_OO, odd_side, 56, T_OO, 3, C_OO)
            swiglu(U_F1, C_F1, T_F1, 3, T_OO, C_OO, 0)
            with act.Fori(1, FCH) as j:
                swiglu(U_F1, C_F1, T_F1, 3, T_OO, C_OO, j)
            for n in range(NCH):
                down(U_D1, T_F1, None, 4, C_D1, n)
            act.activation(root[:, 4, 0:1], eps[:], ACT.Sqrt)
            squares_of(4, NCH - 1, C_D1)
            root_of(4)
            act.wait_ge(rstd_made, 5)
            for h in range(2):
                cols = slice(h * 1024, (h + 1) * 1024)
                act.activation(xs[:, 1, cols], xs[:, 1, cols], ACT.Identity,
                               scale=rstd[:, 4, 0, 1:2]).then_inc(out_act, 1)

        @block.vector
        def _(dve):
            steps = [0]

            def link(ins):
                steps[0] += 1
                ins.then_inc(dve_step, 1)
                dve.wait_ge(dve_step, steps[0])

            def split_lo(h, j=0):
                rows, slot, r0 = half_rows(h), h // 2 % 4, 2 * (h % 2)
                dve.wait_ge(hi_made, h + 1 + j * 16)
                wait(dve, half_used, h - 3 + j * 16)
                dve.tensor_tensor(w_lo[:, h % 4, 0:rows, :], raw[:, slot, r0:r0 + rows, :],
                                  w_hi[:, h % 4, 0:rows, :].bitcast(F32), ALU.subtract).then_inc(lo_made, 1)

            def turn_lo(t, src, hi, lo):
                dve.wait_ge(turn_act, t + 1)
                dve.tensor_tensor(lo.rearrange("p (t c) -> p t c", t=TT), src,
                                  hi.bitcast(F32).rearrange("p (t c) -> p t c", t=TT),
                                  ALU.subtract).then_inc(turn_dve, 1)

            def x_turn_lo(t, norm, kt):
                dve.wait_ge(turn_act, t + 1)
                dve.scalar_tensor_tensor(a_lo[:, kt, :].rearrange("p (t c) -> p t c", t=TT), turn_psum(t),
                                         gain[:, norm, kt:kt + 1],
                                         a_hi[:, kt, :].bitcast(F32).rearrange("p (t c) -> p t c", t=TT),
                                         ALU.mult, ALU.subtract).then_inc(turn_dve, 1)

            def turn_copy(t, src, dst):
                dve.wait_ge(turned, t + 1)
                dve.tensor_copy(dst, src).then_inc(turn_dve, 1)

            def inverse_root(r, root, half, r0, tmp):
                link(dve.reciprocal(r0, root))
                link(dve.tensor_tensor(tmp, r0, r0, ALU.mult))
                link(dve.tensor_tensor(tmp, tmp, half, ALU.mult))
                link(dve.scalar_tensor_tensor(tmp, tmp, 1.5, r0, ALU.subtract, ALU.mult))
                return dve.tensor_scalar(r, tmp, -1.0, None, ALU.mult)

            def half_mean_square(norm):
                link(dve.tensor_scalar(half_ms[:, norm, :], ssum[:, norm, :], 0.5 / D, 0.5 * EPS,
                                       ALU.mult, ALU.add))

            def rstd_of(norm):
                dve.wait_ge(squares, 8 * norm + 8)
                dve.tensor_reduce(ssum[:, norm, :], ssq[:, norm, :, :], AX.X, ALU.add).then_inc(sum_made, 1)
                dve.wait_ge(sum_made, norm + 1)
                half_mean_square(norm)
                dve.wait_ge(root_made, norm + 1)
                link(inverse_root(rstd[:, norm, 0, :], root[:, norm, :], half_ms[:, norm, :],
                                  rstd[:, norm, 1, :], rstd[:, norm, 2, :]))
                link(dve.tensor_scalar(rstd[:, norm, 1, :], rstd[:, norm, 0, :], 0.125, None, ALU.mult))
                dve.tensor_scalar(rstd[:, norm, 2, :], rstd[:, norm, 0, :], 0.5, None,
                                  ALU.mult).then_inc(rstd_made, 1)

            def attend_max(k, gk):
                dve.wait_ge(scores_made, gk + 1)
                wait(dve, probs_made, 4 * gk)
                scores = ps_s
                if gk < 8:
                    dve.wait_ge(params_in, PARAMS)
                    wait(dve, probs_turned, gk)
                    link(dve.tensor_tensor(prob[:], ps_s[:, :, 0:384],
                                           win[:].unsqueeze(1).to_broadcast([P, 2, 384]), ALU.add))
                    scores = prob
                link(dve.tensor_reduce(mx[:, 0, :], scores[:, :, 0:128], AX.X, ALU.max))
                link(dve.tensor_reduce(mx[:, 1, :], scores[:, :, 128:384], AX.X, ALU.max))
                if gk < 8:
                    wait(dve, sinks_made, gk)
                    link(dve.scalar_tensor_tensor(nm[:], mx[:], -1.0, nsink[:, k, :, :], ALU.mult, ALU.min))
                    dve.tensor_tensor(sshift[:], nm[:], sinkv[:, k, :, :], ALU.add).then_inc(max_made, 1)
                else:
                    dve.tensor_scalar(nm[:], mx[:], -1.0, None, ALU.mult).then_inc(max_made, 1)

            def attend_turned(gk):
                dve.wait_ge(probs_turned, gk + 1)
                wait(dve, pv_made, gk)
                dve.tensor_copy(probT[:, 1, :], ps_t[:, 1, 0:384]).then_inc(probT_dve, 1)
                dve.wait_ge(probs_made, 4 * gk + 4)
                if gk < 8:
                    dve.wait_ge(sinks_made, gk + 1)
                    link(dve.tensor_tensor(den[:], psum_p[:], es[:], ALU.add))
                    link(dve.reciprocal(rden[:], den[:]))
                else:
                    link(dve.reciprocal(rden[:], psum_p[:]))

            def attend_out(gk, former_turn):
                dve.wait_ge(pv_made, gk + 1)
                if gk < 7:
                    dve.wait_ge(scores_made, gk + 2)
                if gk == 7:
                    dve.wait_ge(ml_scores, 1)
                wait(dve, turned, former_turn + 1)
                dve.tensor_tensor(yp[:].rearrange("p t (h d) -> p t h d", h=2),
                                  ps_s[:, :, 384:512].rearrange("p t (h d) -> p t h d", h=2),
                                  rden[:].unsqueeze(3).to_broadcast([P, 2, 2, 64]),
                                  ALU.mult).then_inc(pair_made, 1)

            def head_norm(n, heads, y):
                dve.wait_ge(head_root, n)
                n = heads.stop - heads.start
                half, r0, tmp = (hnorm[:, i, 0:n, :] for i in range(3))
                link(dve.tensor_scalar(half, mv[:, heads, :, 1], 0.5, 0.5 * EPS, ALU.mult, ALU.add))
                link(inverse_root(rs[:, heads, :], sd[:, heads, :], half, r0, tmp))
                for h in range(heads.start, heads.stop):
                    for t in range(TT):
                        ins = dve.tensor_scalar(y[:, t, h, :], y[:, t, h, :], mv[:, h, t, 0:1],
                                                rs[:, h, t:t + 1], ALU.subtract, ALU.mult)
                    ins.then_inc(head_normed, 1)

            def even_drain(n):
                c = E_ORDER[n]
                pair = (C_E + n) % 2
                if c >= 7:
                    return
                dve.wait_ge(half_used, 2 * (U_E + 4 * n + 4))
                dve.wait_ge(rstd_made, 1)
                ps = ps_g[:, pair, 1, :]
                r1, r8 = rstd[:, 0, 0, 1:2], rstd[:, 0, 1, 1:2]
                if c == 2:
                    for d in range(2):
                        dve.tensor_scalar(aknat[:, 1, :, d, :], ps[:, 0:256].rearrange("p (h d) -> p h d", d=64),
                                          r1, None, ALU.mult)
                    dve.tensor_scalar(av[:, 1, :], ps[:, 256:512], r1, None, ALU.mult).then_inc(drained[pair], 1)
                elif c in (0, 1):
                    dve.tensor_scalar(stage[:, n % 2, 1, :], ps, r8, None, ALU.mult).then_inc(drained[pair], 1)
                elif c in (3, 4):
                    dve.wait_ge(turned, T_E + 4 + 4 * (n - 2))
                    dve.tensor_scalar(stage[:, n % 2, 1, :], ps, r1, None, ALU.mult).then_inc(drained[pair], 1)
                else:
                    h = 2 * (c - 5)
                    dve.tensor_scalar(mv_sb[:, 1, h:h + 2, 0:256], ps.rearrange("p (h d) -> p h d", h=2),
                                      r1, None, ALU.mult).then_inc(drained[pair], 1)

            def convolve(b):
                dve.wait_ge(turn_act, turn_of(E_TURNS, T_E, "conv", b) + 1)
                dve.wait_ge(turn_dve, turn_of(E_TURNS, T_E, "conv", b) + 1)
                acc = cacc[:, b % 2, :]
                link(dve.tensor_scalar(acc, cbuf[:, 3:3 + S], convp[:, b, 3:4], convp[:, b, 4:5],
                                       ALU.mult, ALU.add))
                for j in (2, 1):
                    link(dve.scalar_tensor_tensor(acc, cbuf[:, j:j + S], convp[:, b, j:j + 1], acc,
                                                  ALU.mult, ALU.add))
                dve.scalar_tensor_tensor(acc, cbuf[:, 0:S], convp[:, b, 0:1], acc,
                                         ALU.mult, ALU.add).then_inc(conv_made, 1)

            def gates(s):
                if s == 4:
                    dve.wait_ge(gates_mm, 1)
                    dve.tensor_copy(gateT[:], ps_s[0:8, 0, 0:S]).then_inc(gates_dve, 1)
                if s == 5:
                    dve.wait_ge(gates_mm, 2)
                    for t in range(TT):
                        ins = dve.scalar_tensor_tensor(gx[:, t, :], ps_s[:, 0, 8 * t:8 * t + 8],
                                                       rstd[:, 0, 0, t:t + 1], gbias[:], ALU.mult, ALU.add)
                        link(ins)
                    dve.scalar_tensor_tensor(gsc[:, 0, :, :], gx[:, :, 4:8], -1.0, gx[:, :, 4:8],
                                             ALU.mult, ALU.min).then_inc(gates_dve, 1)
                if s == 6:
                    e, z, w, p, r = (gsc[:, i, :, :] for i in (1, 2, 7, 5, 6))
                    dve.wait_ge(gates_act, 1)
                    link(dve.tensor_scalar(r, e, 2.0, None, ALU.add))
                    link(dve.reciprocal(r, r))
                    link(dve.tensor_tensor(z, e, r, ALU.mult))
                    link(dve.tensor_tensor(w, z, z, ALU.mult))
                    link(dve.tensor_scalar(p, w, 1.0 / (2 * LOG_TERMS + 1), None, ALU.mult))
                    for i in range(LOG_TERMS - 1, 0, -1):
                        link(dve.scalar_tensor_tensor(p, p, 1.0 / (2 * i + 1), w, ALU.add, ALU.mult))
                    link(dve.scalar_tensor_tensor(p, p, 1.0, z, ALU.add, ALU.mult))
                    link(dve.tensor_tensor(z, p, p, ALU.add))
                    dve.scalar_tensor_tensor(gsc[:, 3, :, :], gx[:, :, 4:8], 0.0, z,
                                             ALU.min, ALU.subtract).then_inc(gates_dve, 1)
                if s == 8:
                    dve.wait_ge(gates_mm, 3)
                    fsum = ps_s[:, 0, 16:24].rearrange("p (t h) -> p t h", t=TT)
                    link(dve.tensor_copy(gsc[:, 5, :, :], fsum))
                    dve.tensor_tensor(gsc[:, 4, :, :], gx[:, :, 0:4], gsc[:, 5, :, :],
                                      ALU.subtract).then_inc(gates_dve, 1)
                if s == 9:
                    dve.wait_ge(gates_mm, 4)
                    dve.wait_ge(zeros_made, 3)
                    link(dve.tensor_copy(cmax[:, 0, P:P + S], ps_s[0:4, 1, 0:S]))
                    link(dve.tensor_scalar(cmax[:, 0, P:P + S], cmax[:, 0, P:P + S], 0.0, None, ALU.max))
                    for j in range(8):
                        a, b, d = j % 2, 1 - j % 2, 1 << j
                        link(dve.tensor_tensor(cmax[:, b, P:P + S], cmax[:, a, P:P + S],
                                               cmax[:, a, P - d:P - d + S], ALU.max))
                    dve.tensor_scalar(negm[:], cmax[:, 0, P:P + S], -1.0, None, ALU.mult).then_inc(gates_dve, 1)
                if s == 10:
                    dve.wait_ge(gates_mm, 5)
                    mnat = ps_s[:, 0, 32:40].rearrange("p (t h) -> p t h", t=TT)
                    dve.tensor_tensor(gsc[:, 6, :, :], gsc[:, 5, :, :], mnat, ALU.add).then_inc(gates_dve, 1)

            def mlstm_out(h):
                dve.wait_ge(ml_out, h + 1)
                link(dve.tensor_copy(den[:, 0, :].unsqueeze(2), ps_t[:, :, 256:257]))
                link(dve.scalar_tensor_tensor(den[:, 1, :], den[:, 0, :], -1.0, den[:, 0, :], ALU.mult, ALU.max))
                link(dve.tensor_tensor(den[:, 0, :], den[:, 1, :], gsc[:, 7, :, h], ALU.max))
                link(dve.reciprocal(rden[:, 0, :], den[:, 0, :]))
                for t in range(TT):
                    ins = dve.tensor_scalar(yB[:, t, h, :], ps_t[:, t, 0:256], rden[:, 0, t:t + 1], None, ALU.mult)
                link(ins)
                for t in range(TT):
                    ins = dve.bn_stats(stats[:, h, t, :], yB[:, t, h, :])
                link(ins)
                for t in range(TT):
                    ins = dve.bn_aggr(mv[:, h, t, :], stats[:, h, t, :])
                ins.then_inc(head_kept, 1)

            def even_side(s):
                if 4 <= s <= 10:
                    gates(s)
                if s - 2 in E_ATT:
                    k = E_ATT.index(s - 2)
                    attend_out(k, turn_of(E_TURNS, T_E, "y", k - 1) if k else -1)
                if s in E_ATT:
                    attend_max(E_ATT.index(s), E_ATT.index(s))
                for i, (slot, kind, b) in enumerate(E_TURNS):
                    if slot != s:
                        continue
                    t = T_E + i
                    src = turn_psum(t)
                    ps_t_settled(dve, 0, s)
                    if kind == "y":
                        if s - 1 in E_ATT:
                            dve.wait_ge(probT_act, E_ATT.index(s - 1) + 1)
                        turn_lo(t, src, y_hi[:, b, :], y_lo[:, b, :])
                    elif kind == "conv":
                        turn_copy(t, src[:, 1, :], cbuf[:, 3 + P:3 + S])
                        convolve(b)
                    else:
                        turn_copy(t, src[:, 1, :], (akT if kind == "k" else aqT)[:, b, P:S])
                if s - 1 in E_ATT:
                    attend_turned(E_ATT.index(s - 1))
                for b in range(8):
                    if s == 18 + 2 * b:
                        dve.wait_ge(tanh_made, b + 1)
                        dve.scalar_tensor_tensor(mqk[:, b, :], cth[:], 1.0, cacc[:, b % 2, :],
                                                 ALU.add, ALU.mult).then_inc(qk_made, 1)
                if s in E_MLSTM:
                    h = E_MLSTM.index(s)
                    dve.wait_ge(ml_weights, 2 * h + 2)
                    wait(dve, ml_out, h)
                    dve.scalar_tensor_tensor(scT[:], ps_s[:, 0, 0:384], MLSTM_SCALE, wgt[:],
                                             ALU.mult, ALU.mult).then_inc(ml_weighted, 1)
                if s - 1 in E_MLSTM:
                    mlstm_out(E_MLSTM.index(s - 1))
                if s < 36 and s % 4 == 3:
                    even_drain(s // 4)
                if s in (33, 35):
                    head_norm((s - 31) // 2, slice(s - 33, s - 31), yB)

            def rope(n):
                dve.wait_ge(odd_in, 32)
                dve.wait_ge(drained[(C_O + n) % 2], drains_after(C_O + n))
                wait(dve, rope_dve, n - 6)
                x = stage[:, n % 2, 1, :].rearrange("p (h a d) -> p h a d", h=4, a=2)
                x1, x2 = x[:, :, 0, :], x[:, :, 1, :]
                cos = trig[:, 0, 1, :].unsqueeze(1).to_broadcast([P, 4, 64])
                sin = trig[:, 1, 1, :].unsqueeze(1).to_broadcast([P, 4, 64])
                dve.tensor_tensor(rtmp[:, 0, 1, :, :], x1, sin, ALU.mult)
                link(dve.tensor_tensor(rtmp[:, 1, 1, :, :], x2, sin, ALU.mult))
                dve.tensor_tensor(x1, x1, cos, ALU.mult)
                link(dve.tensor_tensor(x2, x2, cos, ALU.mult))
                dve.tensor_tensor(x1, x1, rtmp[:, 1, 1, :, :], ALU.subtract)
                dve.tensor_tensor(x2, x2, rtmp[:, 0, 1, :, :], ALU.add).then_inc(rope_dve, 1)

            def odd_drain(n):
                c = O_ORDER[n]
                pair = (C_O + n) % 2
                if c >= 12:
                    return
                dve.wait_ge(half_used, 2 * (U_O + 4 * n + 4))
                dve.wait_ge(rstd_made, 3)
                ps = ps_g[:, pair, 1, :]
                r1, r8 = rstd[:, 2, 0, 1:2], rstd[:, 2, 1, 1:2]
                if c < 4 or 6 <= c < 10:
                    if n in (2, 3, 6, 7, 8, 9):
                        dve.wait_ge(turned, odd_stage_free(n))
                    dve.tensor_scalar(stage[:, n % 2, 1, :], ps, r8 if c < 2 else r1, None,
                                      ALU.mult).then_inc(drained[pair], 1)
                    if c >= 6:
                        rope(n)
                elif c < 6:
                    dve.tensor_scalar(cv[:, 1, (c - 4) * CW:(c - 3) * CW], ps, r1, None,
                                      ALU.mult).then_inc(drained[pair], 1)
                else:
                    dve.tensor_scalar(rv[:, 1, (c - 10) * CW:(c - 9) * CW], ps, r1, None,
                                      ALU.mult).then_inc(drained[pair], 1)

            def odd_side(s):
                if s in O_ATT:
                    attend_max(O_ATT.index(s), 8 + O_ATT.index(s))
                for i, (slot, kind, b) in enumerate(O_TURNS):
                    if slot != s:
                        continue
                    t = T_O + i
                    src = turn_psum(t)
                    ps_t_settled(dve, 1, s)
                    if kind == "y":
                        turn_lo(t, src, y_hi[:, b, :], y_lo[:, b, :])
                    elif kind == "rope":
                        g, h = b // 4, b % 4
                        turn_copy(t, src[:, 1, :], (rqT, rkT)[g % 2][:, 4 * (g // 2) + h, P:S])
                    else:
                        turn_copy(t, src[:, 1, :], (cqT if kind == "q" else ckT)[:, b, P:S])
                if s - 1 in O_ATT:
                    attend_turned(8 + O_ATT.index(s - 1))
                if s - 2 in O_ATT:
                    k = O_ATT.index(s - 2)
                    attend_out(8 + k, turn_of(O_TURNS, T_O, "y", k - 1) if k else -1)
                if s in O_RET:
                    h = O_RET.index(s)
                    dve.wait_ge(decay_in, 16)
                    dve.wait_ge(ret_scores, h + 1)
                    wait(dve, ret_out, h - 1)
                    sc = scD[:, h % 2, :]
                    dve.tensor_tensor(sc[:, 0:256], ps_s[:, h % 2, 0:256], decay[:, h, :], ALU.mult)
                    dve.tensor_tensor(sc[:, 256:384], ps_s[:, h % 2, 256:384], decay[:, h, 0:128],
                                      ALU.mult).then_inc(ret_decayed, 1)
                if s - 1 in O_RET:
                    h = O_RET.index(s - 1)
                    dve.wait_ge(ret_out, h + 1)
                    dve.wait_ge(turn_act, T_O + sum(slot <= s for slot, _, _ in O_TURNS))
                    link(dve.tensor_copy(yD[:, :, h, :], ps_t[:, h % 2, 0:256].rearrange("p (t c) -> p t c", t=TT)))
                    for t in range(TT):
                        ins = dve.bn_stats(stats[:, h, t, :], yD[:, t, h, :])
                    link(ins)
                    for t in range(TT):
                        ins = dve.bn_aggr(mv[:, h, t, :], stats[:, h, t, :])
                    ins.then_inc(head_kept, 1)
                if s < 56 and s % 4 == 3:
                    odd_drain(s // 4)
                if s == 49:
                    head_norm(3, slice(0, 4), yD)
                if s == 55:
                    head_norm(4, slice(4, 8), yD)

            dve.memset(ones[:], 1.0).then_inc(ones_made, 1)
            dve.memset(eps[:], EPS).then_inc(zeros_made, 1)
            dve.memset(cbuf[:, 0:3], 0.0).then_inc(zeros_made, 1)
            dve.memset(cmax[:, :, 0:P], 0.0).then_inc(zeros_made, 1)
            dve.memset(mv_sb[:, :, :, 256:257], 1.0).then_inc(zeros_made, 1)
            dve.wait_ge(first_in, 32)
            for b in range(8):
                x_turn_lo(T_X + b, 0, b)
                if b == 3:
                    split_lo(0)
                    split_lo(1)
            split_lo(2)
            for s in range(36):
                split_ahead(split_lo, U_E + s)
                if s < 2:
                    for b in range(8 + 4 * s, 12 + 4 * s):
                        x_turn_lo(T_X + b, 0, b)
                if s == 3:
                    dve.wait_ge(params_in, PARAMS)
                    dve.tensor_scalar(nsink[:], sinkv[:], -1.0, None, ALU.mult).then_inc(zeros_made, 1)
                    dve.wait_ge(gatew_hi, 1)
                    dve.tensor_tensor(gw_lo[:], gw[:], gw_hi[:].bitcast(F32), ALU.subtract).then_inc(gatew_lo, 1)
                if s == 2:
                    rstd_of(0)
                even_side(s)

            def add_x(u_end, pair, n):
                dve.wait_ge(half_used, 2 * (u_end))
                for t in range(TT):
                    cols = xs[:, t, n * CW:(n + 1) * CW]
                    dve.tensor_tensor(cols, ps_g[:, pair, t, :], cols, ALU.add).then_inc(drained[pair], 1)

            def gain_x(n):
                dve.wait_ge(squares, 8 * 4 + 2 * n + 2)
                dve.wait_ge(final_g_in, 16)
                cols = slice(n * CW, (n + 1) * CW)
                for t in range(TT):
                    dve.tensor_tensor(xs[:, t, cols], xs[:, t, cols], final_gain[:, cols],
                                      ALU.mult).then_inc(x_gained, 1)

            def out_proj(u0, c0, side, late, t0, norm):
                for n in range(NCH):
                    for i in range(4):
                        split_ahead(split_lo, u0 + 4 * n + i)
                        side(late + 4 * n + i)
                        if n >= 1:
                            x_turn_lo(t0 + 4 * (n - 1) + i, norm, 4 * (n - 1) + i)
                    add_x(u0 + 4 * n + 4, (c0 + n) % 2, n)

            def last_x(s, t0, norm):
                if s < 2:
                    for b in (2 * s, 2 * s + 1):
                        x_turn_lo(t0 + 12 + b, norm, 12 + b)
                if s == 2:
                    rstd_of(norm)

            def swiglu(u0, c0, t0, norm, tcx, j):
                for i in range(8):
                    split_ahead(split_lo, u0 + i, j)
                    if isinstance(j, int):
                        last_x(i, tcx, norm)
                    elif i < 4:
                        t = t0 + i + j * 4 - 4
                        dve.wait_ge(turn_act, t + 1)
                        kt = bass.ds(j * 4 + (i - 4), 1)
                        dve.tensor_tensor(h_lo[:, kt, :].rearrange("p a (t c) -> p (a t) c", t=TT),
                                          ring[region[t0 + i]],
                                          h_hi[:, kt, :].bitcast(F32).rearrange("p a (t c) -> p (a t) c", t=TT),
                                          ALU.subtract).then_inc(turn_dve, 1)
                    if i == 7:
                        dve.wait_ge(half_used, 2 * (u0 + 8 + j * 8))
                        dve.wait_ge(rstd_made, norm + 1)
                        dve.wait_ge(drained[c0 % 2], 2 * (c0 // 2) + 2 + j * 2)
                        for t in range(TT):
                            dve.scalar_tensor_tensor(prod[:, t, :], ps_g[:, (c0 + 1) % 2, t, :],
                                                     rstd[:, norm, 0, t:t + 1], silu[:, t, :],
                                                     ALU.mult, ALU.mult).then_inc(drained[(c0 + 1) % 2], 1)

            def down(u0, c0, t0, tcx, norm, n):
                for i in range(12):
                    split_ahead(split_lo, u0 + 12 * n + i)
                    if n == 0 and i < 4:
                        t = t0 + FKT - 4 + i
                        turn_lo(t, turn_psum(t), h_hi[:, FKT - 4 + i, :], h_lo[:, FKT - 4 + i, :])
                    if n >= 1 and i < 4 and tcx is not None:
                        x_turn_lo(tcx + 4 * (n - 1) + i, norm, 4 * (n - 1) + i)
                    if n >= 1 and i == 5 and tcx is None:
                        gain_x(n - 1)
                add_x(u0 + 12 * n + 12, (c0 + n) % 2, n)

            out_proj(U_EO, C_EO, even_side, 36, T_EO, 1)
            swiglu(U_F0, C_F0, T_F0, 1, T_EO, 0)
            with dve.Fori(1, FCH) as j:
                swiglu(U_F0, C_F0, T_F0, 1, T_EO, j)
            for n in range(NCH):
                down(U_D0, C_D0, T_F0, T_D0, 2, n)
            for s in range(56):
                split_ahead(split_lo, U_O + s)
                last_x(s, T_D0, 2)
                odd_side(s)
            out_proj(U_OO, C_OO, odd_side, 56, T_OO, 3)
            swiglu(U_F1, C_F1, T_F1, 3, T_OO, 0)
            with dve.Fori(1, FCH) as j:
                swiglu(U_F1, C_F1, T_F1, 3, T_OO, j)
            for n in range(NCH):
                down(U_D1, C_D1, T_F1, None, 4, n)
            dve.wait_ge(squares, 8 * 4 + 8)
            dve.tensor_reduce(ssum[:, 4, :], ssq[:, 4, :, :], AX.X, ALU.add).then_inc(sum_made, 1)
            gain_x(NCH - 1)
            dve.wait_ge(sum_made, 5)
            half_mean_square(4)
            dve.wait_ge(root_made, 5)
            inverse_root(rstd[:, 4, 0, :], root[:, 4, :], half_ms[:, 4, :], rstd[:, 4, 1, :],
                         rstd[:, 4, 2, :]).then_inc(rstd_made, 1)
            dve.wait_ge(rstd_made, 5)
            dve.wait_ge(x_gained, TT * NCH)
            for h in range(2):
                cols = slice(h * 1024, (h + 1) * 1024)
                dve.tensor_scalar(xs[:, 0, cols], xs[:, 0, cols], rstd[:, 4, 0, 0:1], None,
                                  ALU.mult).then_inc(out_dve, 1)

        @block.gpsimd
        def _(pool):
            steps = [0]

            def link(ins):
                steps[0] += 1
                ins.then_inc(pool_step, 1)
                pool.wait_ge(pool_step, steps[0])

            def gain_gate(cols, g):
                for t in range(TT):
                    ins = pool.tensor_tensor(gfac[:, t, cols], gfac[:, t, cols], g[:, cols], ALU.mult)
                ins.then_inc(gate_made, 1)

            def gated(n, gates, y, h, width):
                pool.wait_ge(head_normed, n + 1)
                pool.wait_ge(gate_made, gates)
                pool.tensor_tensor(y[:, :, h, :], y[:, :, h, :], gfac[:, :, h * width:(h + 1) * width],
                                   ALU.mult).then_inc(head_gated, 1)

            pool.wait_ge(params_in, PARAMS)
            for c in range(2):
                n = 7 + c
                pool.wait_ge(drained[(C_E + n) % 2], 2 * ((C_E + n) // 2) + 2)
                cols = slice(c * CW, (c + 1) * CW)
                link(pool.tensor_scalar(gfac[:, :, cols], gfac[:, :, cols], 1.0, 0.5, ALU.add, ALU.mult))
                gain_gate(cols, gnorm[:])
                for h in (2 * c, 2 * c + 1):
                    gated(h, c + 1, yB, h, 256)
            pool.wait_ge(odd_in, 32)
            for k in range(2):
                pool.wait_ge(bias_in[k % 2], 32 * (k // 2) + 32)
                pool.memset(biasT[0:64, k % 2, :, 0:64], NEG).then_inc(bias_masked, 1)

            def rope(n):
                pool.wait_ge(drained[(C_O + n) % 2], drains_after(C_O + n))
                wait(pool, rope_pool, 2 * (n - 6))
                for pair in (slice(0, 2), slice(2, 4)):
                    x = stage[:, n % 2, 0, :].rearrange("p (h a d) -> p h a d", h=4, a=2)[:, pair, :, :]
                    x1, x2 = x[:, :, 0, :], x[:, :, 1, :]
                    cos = trig[:, 0, 0, :].unsqueeze(1).to_broadcast([P, 2, 64])
                    sin = trig[:, 1, 0, :].unsqueeze(1).to_broadcast([P, 2, 64])
                    x1_sin, x2_sin = rtmp[:, 0, 0, pair, :], rtmp[:, 1, 0, pair, :]
                    pool.tensor_tensor(x1_sin, x1, sin, ALU.mult)
                    link(pool.tensor_tensor(x2_sin, x2, sin, ALU.mult))
                    pool.tensor_tensor(x1, x1, cos, ALU.mult)
                    link(pool.tensor_tensor(x2, x2, cos, ALU.mult))
                    pool.tensor_tensor(x1, x1, x2_sin, ALU.subtract)
                    pool.tensor_tensor(x2, x2, x1_sin, ALU.add).then_inc(rope_pool, 1)

            for k in range(2, 8):
                pool.wait_ge(bias_in[k % 2], 32 * (k // 2) + 32)
                pool.memset(biasT[0:64, k % 2, :, 0:64], NEG).then_inc(bias_masked, 1)
                if k in (4, 5, 6, 7):
                    rope(k + 2)
            for c in range(2):
                n = 12 + c
                pool.wait_ge(drained[(C_O + n) % 2], 2 * ((C_O + n) // 2) + 2)
                pool.wait_ge(odd_in, 48)
                cols = slice(c * CW, (c + 1) * CW)
                gain_gate(cols, gnorm_o[:])
                for h in range(4 * c, 4 * c + 4):
                    gated(4 + h, 3 + c, yD, h, 128)

        @block.tensor
        def _(pe):
            def unit(u, k0, pair, hi, lo, first, last, j=0):
                for h in (2 * u, 2 * u + 1):
                    pe.wait_ge(hi_made, h + 1 + j * 16)
                    pe.wait_ge(lo_made, h + 1 + j * 16)
                    for k in range(half_rows(h)):
                        kt = k0 + 2 * (h % 2) + k
                        end = last and kt == k0 + UNIT_ROWS[u] - 1
                        for t in range(TT):
                            tok = slice(t * P, (t + 1) * P)
                            acc = ps_g[:, pair, t, :]
                            wh, wl = w_hi[:, h % 4, k, :], w_lo[:, h % 4, k, :]
                            pe.matmul(acc, hi[:, kt, tok], wh, start=first and kt == k0, stop=False)
                            pe.matmul(acc, hi[:, kt, tok], wl, start=False, stop=False)
                            ins = pe.matmul(acc, lo[:, kt, tok], wh, start=False, stop=end)
                    ins.then_inc(half_used, 1)

            def chunk_free(chunk):
                wait(pe, drained[chunk % 2], drains_before(chunk))

            def turn(t, src0, src1):
                before = turn_before(t)
                wait(pe, turn_act, before + 1)
                wait(pe, turn_dve, before + 1)
                dst = turn_psum(t)
                pe.transpose(dst[:, 0, :], src0, ident[:])
                pe.transpose(dst[:, 1, :], src1, ident[:]).then_inc(turned, 1)

            def x_turn(t, kt):
                cols = slice(kt * P, (kt + 1) * P)
                turn(t, xs[:, 0, cols], xs[:, 1, cols])

            def operand_ready(t):
                pe.wait_ge(turn_act, t + 1)
                pe.wait_ge(turn_dve, t + 1)

            def attend_pv(gk, v):
                pe.wait_ge(probT_act, gk + 1)
                pe.wait_ge(probT_dve, gk + 1)
                wait(pe, pair_made, gk)
                for hh in range(2):
                    o = slice(384 + 64 * hh, 448 + 64 * hh)
                    pe.matmul(ps_s[:, 0, o], probT[:, hh, 0:128], v(0, hh), start=True, stop=True)
                    pe.matmul(ps_s[:, 1, o], probT[:, hh, 128:256], v(0, hh), start=True, stop=False)
                    ins = pe.matmul(ps_s[:, 1, o], probT[:, hh, 256:384], v(1, hh), start=False, stop=True)
                ins.then_inc(pv_made, 1)

            def attend_turn(gk):
                pe.wait_ge(probs_made, 4 * gk + 4)
                wait(pe, probT_act, gk)
                wait(pe, probT_dve, gk)
                for hh in range(2):
                    for b in range(3):
                        cols = slice(b * P, (b + 1) * P)
                        ins = pe.transpose(ps_t[:, hh, cols], prob[:, hh, cols], ident[:])
                ins.then_inc(probs_turned, 1)

            def even_scores(k):
                wait(pe, probs_made, 4 * k)
                pe.wait_ge(gates_dve, 6)
                operand_ready(turn_of(E_TURNS, T_E, "q", k))
                kv = k // 2
                for hh in range(2):
                    half = slice(64 * hh, 64 * hh + 64)
                    s = ps_s[:, hh, :]
                    pe.matmul(s[:, 0:128], aqT[half, k, 0:P], akT[half, kv, 0:P], start=True, stop=True)
                    ins = pe.matmul(s[:, 128:384], aqT[half, k, P:S], akT[half, kv, :], start=True, stop=True)
                ins.then_inc(scores_made, 1)

            def gates(s):
                if s == 4:
                    pe.wait_ge(gatew_lo, 1)
                    o = ps_s[0:8, 0, 0:S]
                    for k in range(KT):
                        pe.matmul(o, gw_hi[:, k, :], a_hi[:, k, :], start=k == 0, stop=False)
                        pe.matmul(o, gw_hi[:, k, :], a_lo[:, k, :], start=False, stop=False)
                        ins = pe.matmul(o, gw_lo[:, k, :], a_hi[:, k, :], start=False, stop=k == KT - 1)
                    ins.then_inc(gates_mm, 1)
                if s == 5:
                    pe.wait_ge(gates_dve, 1)
                    for t in range(TT):
                        ins = pe.transpose(ps_s[:, 0, 8 * t:8 * t + 8], gateT[:, t * P:(t + 1) * P],
                                           ident[0:8, 0:8])
                    ins.then_inc(gates_mm, 1)
                if s == 8:
                    pe.wait_ge(gates_dve, 3)
                    pe.wait_ge(ones_made, 1)
                    pe.matmul(ps_s[:, 0, 16:20], upper[:], gsc[:, 3, 0, :], start=True, stop=True)
                    pe.matmul(ps_s[:, 0, 20:24], ones[:], gsc[:, 3, 0, :], start=True, stop=False)
                    pe.matmul(ps_s[:, 0, 20:24], upper[:], gsc[:, 3, 1, :], start=False,
                              stop=True).then_inc(gates_mm, 1)
                if s == 9:
                    pe.wait_ge(gates_dve, 4)
                    pe.transpose(ps_s[0:4, 1, 0:P], gsc[:, 4, 0, :], ident[:])
                    pe.transpose(ps_s[0:4, 1, P:S], gsc[:, 4, 1, :], ident[:]).then_inc(gates_mm, 1)
                if s == 10:
                    pe.wait_ge(gates_dve, 5)
                    for t in range(TT):
                        ins = pe.transpose(ps_s[:, 0, 32 + 4 * t:36 + 4 * t],
                                           cmax[:, 0, P + t * P:P + (t + 1) * P], ident[0:4, 0:4])
                    ins.then_inc(gates_mm, 1)

            def mlstm_scores(h):
                pe.wait_ge(qk_made, 5 + h)
                pe.wait_ge(gates_act, 2)
                pe.wait_ge(consts_made, 2)
                wait(pe, probs_made, 32)
                pe.wait_ge(pair_made, 8 if h else 7)
                wait(pe, ml_weighted, h)
                q, kk = mqk[:, h, :], mqk[:, 4 + h, :]
                pe.matmul(ps_s[:, 0, 0:256], kk[:, 0:P], q, start=True, stop=True)
                pe.matmul(ps_s[:, 0, 256:384], kk[:, P:S], q[:, P:S], start=True, stop=True)
                pe.matmul(ps_s[:, 1, 0:128], selr[:, h, :], negm[:, 0:P], start=True, stop=False)
                pe.matmul(ps_s[:, 1, 0:128], ident_b[:], tri_b[:], start=False, stop=True)
                pe.matmul(ps_s[:, 1, 128:256], selr[:, h, :], negm[:, P:S], start=True, stop=True)
                pe.matmul(ps_s[:, 1, 256:384], selr[:, h, :], negm[:, P:S], start=True, stop=False)
                pe.matmul(ps_s[:, 1, 256:384], ident_b[:], tri_b[:], start=False,
                          stop=True).then_inc(ml_scores, 1)

            def mlstm_values(h):
                pe.wait_ge(ml_weighted, h + 1)
                pe.wait_ge(zeros_made, 4)
                pe.wait_ge(drained[(5 + h // 2) % 2], drains_after(5 + h // 2))
                wait(pe, probT_act, 8)
                wait(pe, probT_dve, 8)
                wait(pe, head_kept, h)
                v0, v1 = mv_sb[:, 0, h, 0:257], mv_sb[:, 1, h, 0:257]
                pe.matmul(ps_t[:, 0, 0:257], scT[:, 0:128], v0, start=True, stop=True)
                pe.matmul(ps_t[:, 1, 0:257], scT[:, 128:256], v0, start=True, stop=False)
                pe.matmul(ps_t[:, 1, 0:257], scT[:, 256:384], v1, start=False, stop=True).then_inc(ml_out, 1)

            def even_side(s):
                for i, (slot, kind, b) in enumerate(E_TURNS):
                    if slot != s:
                        continue
                    t = T_E + i
                    cols = slice((b % 4) * P, (b % 4 + 1) * P)
                    if slot < LATE[0]:
                        ps_t_free(pe, 0, s)
                    if kind == "k":
                        pe.wait_ge(drained[0], 2)
                        turn(t, aknat[:, 0, b, :, :].rearrange("p a d -> p (a d)"),
                             aknat[:, 1, b, :, :].rearrange("p a d -> p (a d)"))
                    elif kind in ("q", "conv"):
                        n = 1 + b // 4 if kind == "q" else 3 + b // 4
                        pe.wait_ge(drained[n % 2], 2 * (n // 2) + 2)
                        turn(t, stage[:, n % 2, 0, cols], stage[:, n % 2, 1, cols])
                    elif b < 8:
                        pe.wait_ge(pair_made, b + 1)
                        turn(t, yp[:, 0, :], yp[:, 1, :])
                    else:
                        h, half = (b - 8) // 2, slice((b % 2) * P, (b % 2 + 1) * P)
                        pe.wait_ge(head_gated, h + 1)
                        turn(t, yB[:, 0, h, half], yB[:, 1, h, half])
                gates(s)
                if s - 1 in E_ATT + E_MLSTM:
                    ps_t_free(pe, 0, s)
                if s - 2 in E_ATT:
                    k = E_ATT.index(s - 2)
                    attend_pv(k, lambda t, hh: av[:, t, (k // 2) * 64:(k // 2) * 64 + 64])
                if s - 1 in E_ATT:
                    attend_turn(E_ATT.index(s - 1))
                if s in E_ATT:
                    even_scores(E_ATT.index(s))
                if s - 1 in E_MLSTM:
                    mlstm_values(E_MLSTM.index(s - 1))
                if s in E_MLSTM:
                    mlstm_scores(E_MLSTM.index(s))

            def odd_scores(k):
                wait(pe, probs_made, 4 * (8 + k))
                pe.wait_ge(pair_made, 8 + k)
                pe.wait_ge(bias_masked, k + 1)
                pe.wait_ge(odd_in, 32)
                operand_ready(turn_of(O_TURNS, T_O, "k", k))
                for hh in range(2):
                    half = slice(64 * hh, 64 * hh + 64)
                    s, b = ps_s[:, hh, :], biasT[:, k % 2, hh, :]
                    pe.matmul(s[:, 0:128], b[:, 0:P], flip[:], start=True, stop=False)
                    pe.matmul(s[:, 0:128], cqT[half, k, 0:P], ckT[half, k, 0:P], start=False, stop=True)
                    pe.matmul(s[:, 128:256], b[:, P:S], flip[:], start=True, stop=False)
                    pe.matmul(s[:, 256:384], b[:, 0:P], flip[:], start=False, stop=False)
                    ins = pe.matmul(s[:, 128:384], cqT[half, k, P:S], ckT[half, k, :], start=False, stop=True)
                ins.then_inc(scores_made, 1)

            def retention_scores(h):
                operand_ready(turn_of(O_TURNS, T_O, "rope", 4 + h if h < 4 else 8 + h))
                wait(pe, probs_made, 64)
                pe.wait_ge(pair_made, 16)
                wait(pe, ret_decayed, h - 1)
                pe.matmul(ps_s[:, h % 2, 0:256], rkT[:, h, 0:P], rqT[:, h, :], start=True, stop=True)
                pe.matmul(ps_s[:, h % 2, 256:384], rkT[:, h, P:S], rqT[:, h, P:S], start=True,
                          stop=True).then_inc(ret_scores, 1)

            def retention_values(h):
                pe.wait_ge(ret_decayed, h + 1)
                pe.wait_ge(drained[(C_O + 10 + h // 4) % 2], 2 * ((C_O + 10 + h // 4) // 2) + 2)
                wait(pe, probT_act, 16)
                wait(pe, probT_dve, 16)
                wait(pe, head_kept, 4 + h - 1)
                sc, o = scD[:, h % 2, :], ps_t[:, h % 2, :]
                v = slice(h * P, (h + 1) * P)
                pe.matmul(o[:, 0:128], sc[:, 0:128], rv[:, 0, v], start=True, stop=True)
                pe.matmul(o[:, 128:256], sc[:, 128:256], rv[:, 0, v], start=True, stop=False)
                pe.matmul(o[:, 128:256], sc[:, 256:384], rv[:, 1, v], start=False, stop=True).then_inc(ret_out, 1)

            def odd_side(s):
                for i, (slot, kind, b) in enumerate(O_TURNS):
                    if slot != s:
                        continue
                    t = T_O + i
                    cols = slice((b % 4) * P, (b % 4 + 1) * P)
                    if slot < LATE[1]:
                        ps_t_free(pe, 1, s)
                    if kind in ("q", "k"):
                        n = 2 * (b // 4) + (kind == "k")
                        pe.wait_ge(drained[(C_O + n) % 2], 2 * ((C_O + n) // 2) + 2)
                        turn(t, stage[:, n % 2, 0, cols], stage[:, n % 2, 1, cols])
                    elif kind == "rope":
                        n = 6 + b // 4
                        pe.wait_ge(rope_pool, b // 2 + 1)
                        pe.wait_ge(rope_dve, b // 4 + 1)
                        turn(t, stage[:, n % 2, 0, cols], stage[:, n % 2, 1, cols])
                    elif b < 8:
                        pe.wait_ge(pair_made, 8 + b + 1)
                        turn(t, yp[:, 0, :], yp[:, 1, :])
                    else:
                        pe.wait_ge(head_gated, 4 + b - 8 + 1)
                        turn(t, yD[:, 0, b - 8, :], yD[:, 1, b - 8, :])
                if s - 1 in O_ATT + O_RET:
                    ps_t_free(pe, 1, s)
                if s - 2 in O_ATT:
                    k = O_ATT.index(s - 2)
                    n = C_O + 4 + k // 4
                    pe.wait_ge(drained[n % 2], drains_after(n))
                    attend_pv(8 + k, lambda t, hh: cv[:, t, (2 * k + hh) * 64:(2 * k + hh) * 64 + 64])
                if s - 1 in O_ATT:
                    attend_turn(8 + O_ATT.index(s - 1))
                if s in O_ATT:
                    odd_scores(O_ATT.index(s))
                if s - 1 in O_RET:
                    retention_values(O_RET.index(s - 1))
                if s in O_RET:
                    retention_scores(O_RET.index(s))

            def keep_warm(count):
                for _ in range(count):
                    pe.matmul(ps_g[:, 1, 1, 0:P], ones[:], ones[:], start=True, stop=True)

            pe.wait_ge(ones_made, 1)
            keep_warm(WARM_UP[0])
            pe.wait_ge(first_in, 32)
            for b in range(8):
                if b % 4 == 0:
                    pe.wait_ge(x_in[b // 4], 16)
                x_turn(T_X + b, b)
                if b % 4 == 3:
                    keep_warm(WARM_UP[1 + b // 4])
            for s in range(36):
                if s % 4 == 0:
                    chunk_free(C_E + s // 4)
                if s < 4:
                    operand_ready(T_X + 4 * s + 3)
                unit(U_E + s, 4 * (s % 4), (C_E + s // 4) % 2, a_hi, a_lo, s % 4 == 0, s % 4 == 3)
                if s < 2:
                    pe.wait_ge(x_in[s + 2], 16)
                    for b in range(8 + 4 * s, 12 + 4 * s):
                        x_turn(T_X + b, b)
                even_side(s)

            def out_proj(u0, c0, turns, ty0, side, late, t0, cx):
                for n in range(NCH):
                    chunk_free(c0 + n)
                    for i in range(4):
                        if n == 0:
                            operand_ready(turn_of(turns, ty0, "y", 4 * i + 3))
                        unit(u0 + 4 * n + i, 4 * i, (c0 + n) % 2, y_hi, y_lo, i == 0, i == 3)
                        side(late + 4 * n + i)
                        if n >= 1:
                            x_ready(pe, cx, n)
                            x_turn(t0 + 4 * (n - 1) + i, 4 * (n - 1) + i)

            def last_x(s, t0, cx):
                if s < 2:
                    for b in (2 * s, 2 * s + 1):
                        x_ready(pe, cx, NCH)
                        x_turn(t0 + 12 + b, 12 + b)

            def swiglu(u0, c0, t0, tcx, cx, j):
                for i in range(8):
                    chunk = c0 + i // 4
                    if i % 4 == 0:
                        if isinstance(j, int):
                            chunk_free(chunk)
                        else:
                            pe.wait_ge(drained[chunk % 2], 2 * (chunk // 2) + j * 2)
                    if isinstance(j, int) and i < 4:
                        operand_ready(tcx + 4 * i + 3)
                    unit(u0 + i, 4 * (i % 4), chunk % 2, a_hi, a_lo, i % 4 == 0, i % 4 == 3, j)
                    if isinstance(j, int):
                        last_x(i, tcx, cx)
                    elif i < 4:
                        pe.wait_ge(drained[(c0 + 1) % 2], 2 * ((c0 + 1) // 2) + j * 2)
                        pe.wait_ge(turn_act, t0 + i - 7 + j * 4)
                        pe.wait_ge(turn_dve, t0 + i - 7 + j * 4)
                        dst = ring[region[t0 + i]]
                        cols = slice(i * P, (i + 1) * P)
                        pe.transpose(dst[:, 0, :], prod[:, 0, cols], ident[:])
                        pe.transpose(dst[:, 1, :], prod[:, 1, cols], ident[:]).then_inc(turned, 1)

            def down(u0, c0, t0, tcx, cx, n):
                chunk_free(c0 + n)
                for i in range(12):
                    if n == 0:
                        operand_ready(t0 + STARTS_DOWN[i] + UNITS_DOWN[i] - 1)
                    unit(u0 + 12 * n + i, STARTS_DOWN[i], (c0 + n) % 2, h_hi, h_lo,
                         i == 0, i == 11)
                    if n == 0 and i < 4:
                        pe.wait_ge(drained[(c0 - 1) % 2], drains_before(c0 + 1))
                        cols = slice(i * P, (i + 1) * P)
                        turn(t0 + FKT - 4 + i, prod[:, 0, cols], prod[:, 1, cols])
                    if n >= 1 and i < 4 and tcx is not None:
                        x_ready(pe, cx, n)
                        x_turn(tcx + 4 * (n - 1) + i, 4 * (n - 1) + i)

            out_proj(U_EO, C_EO, E_TURNS, T_E, even_side, 36, T_EO, C_EO)
            swiglu(U_F0, C_F0, T_F0, T_EO, C_EO, 0)
            with pe.Fori(1, FCH) as j:
                swiglu(U_F0, C_F0, T_F0, T_EO, C_EO, j)
            for n in range(NCH):
                down(U_D0, C_D0, T_F0, T_D0, C_D0, n)
            for s in range(56):
                if s % 4 == 0:
                    chunk_free(C_O + s // 4)
                if s < 4:
                    operand_ready(T_D0 + 4 * s + 3)
                unit(U_O + s, 4 * (s % 4), (C_O + s // 4) % 2, a_hi, a_lo, s % 4 == 0, s % 4 == 3)
                last_x(s, T_D0, C_D0)
                odd_side(s)
            out_proj(U_OO, C_OO, O_TURNS, T_O, odd_side, 56, T_OO, C_OO)
            swiglu(U_F1, C_F1, T_F1, T_OO, C_OO, 0)
            with pe.Fori(1, FCH) as j:
                swiglu(U_F1, C_F1, T_F1, T_OO, C_OO, j)
            for n in range(NCH):
                down(U_D1, C_D1, T_F1, None, C_D1, n)


def constants():
    i = np.arange(P)
    q, k = np.meshgrid(i, np.arange(S), indexing="ij")
    chunk_q, chunk_k = (q + P) // 64, k // 64
    ident = np.eye(P)
    upper = np.triu(np.ones((P, P)))
    win0 = np.where(i[:, None] // 64 >= i[None, :] // 64, 0.0, NEG)
    win1 = np.where((chunk_k <= chunk_q) & (chunk_k >= chunk_q - 1), 0.0, NEG)
    tri = np.where(i[None, :] >= i[:, None], 0.0, NEG)
    inv = np.float32(10000.0) ** (-np.arange(0, 128, 2, dtype=np.float32) / np.float32(128))
    ang = (np.arange(S, dtype=np.float32)[:, None] * inv[None, :]).astype(np.float64)
    trig = [f(ang).reshape(TT, P, 64).transpose(1, 0, 2).reshape(P, TT * 64) for f in (np.cos, np.sin)]
    const = np.concatenate([ident, upper, win0, win1, tri] + trig + [ident[::-1]], axis=1).astype(np.float32)
    gamma = 1.0 - 2.0 ** (-5.0 - np.arange(8))
    rel = np.arange(S)[None, None, :] - i[:, None, None]
    decay = np.where(rel >= 0, gamma[None, :, None] ** np.maximum(rel, 0), 0.0) * 128.0 ** -0.5
    sel = np.zeros((4, 4, P))
    for h in range(4):
        sel[h, h, :] = 1.0
    return const, decay.reshape(P, 8 * S).astype(np.float32), sel.astype(np.float32)


def kernel(x, ln_mix_g, ln_ffn_g, even_w_in, even_w_out, a_sinks, b_conv_w, b_conv_b, b_igate_bias,
           b_fgate_bias, b_norm_g, odd_w_in, odd_w_out, c_rel_bias, d_norm_g, ffn_w_gate, ffn_w_up,
           ffn_w_down, final_g):
    import numpy as _np
    import concourse.bacc as _bacc
    from concourse import mybir as _mybir
    from concourse.bass_utils import run_bass_kernel_spmd as _run

    def arr(a):
        return _np.ascontiguousarray(a)

    const, decay, sel = constants()
    gains = _np.stack([ln_mix_g[0], ln_ffn_g[0], ln_mix_g[1], ln_ffn_g[1]])
    conv = _np.concatenate([_np.asarray(b_conv_w[0]), _np.asarray(b_conv_b)], axis=0)
    rel = _np.asarray(c_rel_bias[0])
    rel = _np.concatenate([rel[:, 1:], _np.repeat(rel[:, 256:257], 127, axis=1)], axis=1)
    arrays = {
        "x": arr(_np.asarray(x).reshape(S, D)),
        "gains": arr(gains.reshape(4, KT, P).transpose(2, 0, 1)),
        "final_g": arr(final_g),
        "w_e": arr(_np.asarray(even_w_in)[0]),
        "w_eo": arr(_np.asarray(even_w_out)[0]),
        "w_o": arr(_np.asarray(odd_w_in)[0]),
        "w_oo": arr(_np.asarray(odd_w_out)[0]),
        "w_gate": arr(ffn_w_gate),
        "w_up": arr(ffn_w_up),
        "w_down": arr(ffn_w_down),
        "sinks": arr(_np.repeat(_np.asarray(a_sinks).reshape(8, 1, 2), 2, axis=1)),
        "conv": arr(conv.reshape(5, 8, P).transpose(2, 1, 0)),
        "gate_bias": arr(_np.concatenate([_np.asarray(b_igate_bias)[0], _np.asarray(b_fgate_bias)[0]])),
        "b_norm_g": arr(_np.asarray(b_norm_g)[0]),
        "d_norm_g": arr(_np.asarray(d_norm_g)[0]),
        "rel": arr(rel),
        "const": const,
        "dtab": decay,
        "sel": sel,
    }
    nc = _bacc.Bacc("TRN2", target_bir_lowering=False, num_devices=1, dynamic_dma_scratch_size=1024)
    aps = {n: nc.dram_tensor(n, a.shape, _mybir.dt.from_np(a.dtype), kind="ExternalInput").ap()
           for n, a in arrays.items()}
    out = nc.dram_tensor("out", (S, D), _mybir.dt.float32, kind="ExternalOutput").ap()
    build(nc, out=out, **aps)
    r = _run(nc, [arrays], core_ids=[0])
    return r.results[0]["out"].reshape(1, S, D)
```
